# Optimizing a Trainium2 kernel written in Bass

```python
import math
import jax, jax.numpy as jnp
from jax import lax
import numpy as np

D_MODEL = 1024
BATCH = 1
SEQ = 512
DEPTH = 2

N_EVEN = (DEPTH + 1) // 2
N_ODD = DEPTH // 2

D_FF = 2816

MIX_WIDTH = D_MODEL
ATTN_WIDTH = MIX_WIDTH // 2
DIFF_HEADS = 4
DIFF_HEAD_DIM = ATTN_WIDTH // (2 * DIFF_HEADS)
DIFF_V_DIM = 2 * DIFF_HEAD_DIM
POOL_WIDTH = MIX_WIDTH - ATTN_WIDTH
POOL_GROUPS = 4
POOL_GROUP_DIM = POOL_WIDTH // POOL_GROUPS
POOL_WINDOWS = (2, 4, 8, 16)
EVEN_IN = 3 * ATTN_WIDTH + POOL_WIDTH

CONV_WIDTH = 3
CONV_DIM = D_MODEL

Q_BLOCK = 128
EPS = 1e-6

kernel_name = "hybrid_diffattn_pool_shortconv_macaron"

def rms_norm(x, g):
    xf = x.astype(jnp.float32)
    y = xf * lax.rsqrt(jnp.mean(xf * xf, axis=-1, keepdims=True) + EPS)
    return (y * g.astype(jnp.float32)).astype(x.dtype)

def swiglu(h, w_gate, w_up, w_down):
    return (jax.nn.silu(h @ w_gate) * (h @ w_up)) @ w_down

def diff_attention(q, k, v, lam):
    S = q.shape[1]
    scale = DIFF_HEAD_DIM ** -0.5
    outs = []
    for start in range(0, S, Q_BLOCK):
        end = min(start + Q_BLOCK, S)
        qb = q[:, start:end]
        kb = k[:, :end]
        vb = v[:, :end]
        s = jnp.einsum('bqhcd,bkhcd->bhcqk', qb, kb).astype(jnp.float32) * scale
        qpos = start + jnp.arange(end - start)
        kpos = jnp.arange(end)
        mask = qpos[:, None] >= kpos[None, :]
        s = jnp.where(mask, s, -jnp.inf)
        p = jax.nn.softmax(s, axis=-1)
        w = p[:, :, 0] - lam * p[:, :, 1]
        outs.append(jnp.einsum('bhqk,bkhe->bqhe', w.astype(vb.dtype), vb))
    return jnp.concatenate(outs, axis=1)

def multiscale_pool(u, w_pool, pool_scale):
    B, S, G, C = u.shape
    uf = u.astype(jnp.float32)
    cs = jnp.cumsum(uf, axis=1)
    cs0 = jnp.concatenate([jnp.zeros((B, 1, G, C), jnp.float32), cs], axis=1)
    win = jnp.array(POOL_WINDOWS, dtype=jnp.int32)
    t = jnp.arange(S, dtype=jnp.int32)
    lo = jnp.maximum(t[:, None] + 1 - win[None, :], 0)
    count = jnp.minimum(t[:, None] + 1, win[None, :]).astype(jnp.float32)
    lo_vals = cs0[:, lo, jnp.arange(G)[None, :]]
    mean = (cs0[:, 1:] - lo_vals) / count[None, :, :, None]
    pooled = (mean - uf).astype(u.dtype)
    y = jnp.einsum('bsgc,gcd->bsgd', pooled, w_pool)
    return y * pool_scale.reshape(G, C)

def even_mixer(h, w_in, w_out, q_gain, k_gain, subln_gain, lq1, lk1, lq2, lk2,
               w_pool, pool_scale, lam_init):
    B, S, _ = h.shape
    proj = h @ w_in
    q = proj[..., :ATTN_WIDTH].reshape(B, S, DIFF_HEADS, 2, DIFF_HEAD_DIM)
    k = proj[..., ATTN_WIDTH:2 * ATTN_WIDTH].reshape(B, S, DIFF_HEADS, 2, DIFF_HEAD_DIM)
    v = proj[..., 2 * ATTN_WIDTH:3 * ATTN_WIDTH].reshape(B, S, DIFF_HEADS, DIFF_V_DIM)
    u = proj[..., 3 * ATTN_WIDTH:].reshape(B, S, POOL_GROUPS, POOL_GROUP_DIM)
    q = rms_norm(q, q_gain)
    k = rms_norm(k, k_gain)
    lam = (jnp.exp(jnp.sum(lq1.astype(jnp.float32) * lk1.astype(jnp.float32)))
           - jnp.exp(jnp.sum(lq2.astype(jnp.float32) * lk2.astype(jnp.float32)))
           + lam_init)
    o = diff_attention(q, k, v, lam)
    o = rms_norm(o, subln_gain) * (1.0 - lam_init)
    p = multiscale_pool(u, w_pool, pool_scale)
    y = jnp.concatenate([o.reshape(B, S, ATTN_WIDTH), p.reshape(B, S, POOL_WIDTH)], axis=-1)
    return y @ w_out

def odd_mixer(h, w_in, conv_w, w_out):
    bch = h @ w_in
    b_gate = bch[..., :CONV_DIM]
    c_gate = bch[..., CONV_DIM:2 * CONV_DIM]
    hh = bch[..., 2 * CONV_DIM:]
    z = c_gate * hh
    kern = conv_w.reshape(CONV_WIDTH, 1, CONV_DIM).astype(z.dtype)
    z = lax.conv_general_dilated(z, kern, window_strides=(1,),
                                 padding=[(CONV_WIDTH - 1, 0)],
                                 dimension_numbers=('NWC', 'WIO', 'NWC'),
                                 feature_group_count=CONV_DIM)
    return (b_gate * z) @ w_out

def setup_inputs(seed: int = 0) -> dict:
    key = jax.random.key(seed)
    ks = iter(jax.random.split(key, 32))
    f32 = jnp.float32

    def nrm(shape, fan_in):
        return jax.random.normal(next(ks), shape, f32) * (fan_in ** -0.5)

    def gain(shape):
        return jnp.ones(shape, f32) + 0.05 * jax.random.normal(next(ks), shape, f32)

    return {
        "x": jax.random.normal(next(ks), (BATCH, SEQ, D_MODEL), f32),
        "ffn1_norm": gain((DEPTH, D_MODEL)),
        "ffn1_w_gate": nrm((DEPTH, D_MODEL, D_FF), D_MODEL),
        "ffn1_w_up": nrm((DEPTH, D_MODEL, D_FF), D_MODEL),
        "ffn1_w_down": nrm((DEPTH, D_FF, D_MODEL), D_FF),
        "ffn2_norm": gain((DEPTH, D_MODEL)),
        "ffn2_w_gate": nrm((DEPTH, D_MODEL, D_FF), D_MODEL),
        "ffn2_w_up": nrm((DEPTH, D_MODEL, D_FF), D_MODEL),
        "ffn2_w_down": nrm((DEPTH, D_FF, D_MODEL), D_FF),
        "mix_norm": gain((DEPTH, D_MODEL)),
        "even_w_in": nrm((N_EVEN, D_MODEL, EVEN_IN), D_MODEL),
        "even_w_out": nrm((N_EVEN, MIX_WIDTH, D_MODEL), MIX_WIDTH),
        "q_gain": gain((N_EVEN, DIFF_HEAD_DIM)),
        "k_gain": gain((N_EVEN, DIFF_HEAD_DIM)),
        "subln_gain": gain((N_EVEN, DIFF_V_DIM)),
        "lambda_q1": 0.1 * jax.random.normal(next(ks), (N_EVEN, DIFF_HEAD_DIM), f32),
        "lambda_k1": 0.1 * jax.random.normal(next(ks), (N_EVEN, DIFF_HEAD_DIM), f32),
        "lambda_q2": 0.1 * jax.random.normal(next(ks), (N_EVEN, DIFF_HEAD_DIM), f32),
        "lambda_k2": 0.1 * jax.random.normal(next(ks), (N_EVEN, DIFF_HEAD_DIM), f32),
        "w_pool": nrm((N_EVEN, POOL_GROUPS, POOL_GROUP_DIM, POOL_GROUP_DIM), POOL_GROUP_DIM),
        "pool_scale": gain((N_EVEN, POOL_WIDTH)),
        "odd_w_in": nrm((N_ODD, D_MODEL, 3 * CONV_DIM), D_MODEL),
        "conv_w": nrm((N_ODD, CONV_WIDTH, CONV_DIM), CONV_WIDTH),
        "odd_w_out": nrm((N_ODD, CONV_DIM, D_MODEL), CONV_DIM),
    }

def reference(x, ffn1_norm, ffn1_w_gate, ffn1_w_up, ffn1_w_down,
              ffn2_norm, ffn2_w_gate, ffn2_w_up, ffn2_w_down,
              mix_norm, even_w_in, even_w_out, q_gain, k_gain, subln_gain,
              lambda_q1, lambda_k1, lambda_q2, lambda_k2, w_pool, pool_scale,
              odd_w_in, conv_w, odd_w_out):
    for l in range(DEPTH):
        x = x + 0.5 * swiglu(rms_norm(x, ffn1_norm[l]), ffn1_w_gate[l], ffn1_w_up[l], ffn1_w_down[l])
        h = rms_norm(x, mix_norm[l])
        i = l // 2
        if l % 2 == 0:
            lam_init = 0.8 - 0.6 * math.exp(-0.3 * l)
            x = x + even_mixer(h, even_w_in[i], even_w_out[i], q_gain[i], k_gain[i],
                               subln_gain[i], lambda_q1[i], lambda_k1[i],
                               lambda_q2[i], lambda_k2[i], w_pool[i], pool_scale[i],
                               lam_init)
        else:
            x = x + odd_mixer(h, odd_w_in[i], conv_w[i], odd_w_out[i])
        x = x + 0.5 * swiglu(rms_norm(x, ffn2_norm[l]), ffn2_w_gate[l], ffn2_w_up[l], ffn2_w_down[l])
    return x


_drawn_inputs = setup_inputs


def setup_inputs(seed=0):
    import zlib

    import numpy as np

    out = dict(_drawn_inputs(seed))
    spreads = {}
    factors = {'lambda_k2': 3.644}
    for name, (base, spread) in spreads.items():
        noise = np.random.default_rng([zlib.crc32(name.encode()), seed]).standard_normal(out[name].shape)
        drawn = base * np.exp(spread * noise) if base else spread * noise
        out[name] = __import__('jax').numpy.asarray(drawn.astype(out[name].dtype))
    for name, factor in factors.items():
        out[name] = (out[name] * factor).astype(out[name].dtype)
    return out
```

```python
from contextlib import ExitStack

import concourse.bass as bass
from concourse import mybir

F32 = mybir.dt.float32
F32R = mybir.dt.float32r
ALU = mybir.AluOpType
ACT = mybir.ActivationFunctionType
AX_X = mybir.AxisListType.X

P = 128
D = 1024
T = 512
FF = 2816
NB = D // P
TB = T // P
FT = FF // P
HEADS = 4
HD = 64
WINDOWS = (2, 4, 8, 16)
CONV = 3
EPS = 1e-6
LAM_INIT = 0.8 - 0.6
MASKED = -1e30
RING = 4
UNIT = 8 * P
PAD = 8

DOWN_UNITS = (6, 6, 5, 5)
DOWN_FIRST = (0, 6, 12, 17)


GATE_BANKS = (0, 2)
RES_BANKS = (4, 5)
GROUP_BANKS = ((0, 1, 2), (3, 6, 7))
STAT_BANK = 6
SPREAD_BANK = 7
Q_BANK = U_BANK = 0
K_BANK = POOL_BANK = 1
V_BANK = 2
SCORE_BANKS = (2, 4)
OUT_BANKS = (6, 7)

WT0, Y0, V0, Q0, K0, POOLED, WPOOL = 1, 5, 13, 17, 19, 20, 21
NORM_ROWS = 6 * NB
COL_CONV = NORM_ROWS
COL_PSCALE = COL_CONV + CONV * NB
COL_QGAIN = COL_PSCALE + HEADS
COL_KGAIN, COL_SUB, N_COLS = COL_QGAIN + 1, COL_QGAIN + 2, COL_QGAIN + 3


def build(nc, x_in, ffn1_norm, ffn1_w_gate, ffn1_w_up, ffn1_w_down, ffn2_norm, ffn2_w_gate,
          ffn2_w_up, ffn2_w_down, mix_norm, even_w_in, even_w_out, q_gain, k_gain, subln_gain,
          lambda_q1, lambda_k1, lambda_q2, lambda_k2, w_pool, pool_scale, odd_w_in, conv_w,
          odd_w_out, out):
    start, rounds = {}, 0
    for name, units in (("ffn0", 2 * FT + 4 * NB), ("even", 4 + 3 * HEADS), ("even_out", NB),
                        ("ffn1", 2 * FT + 4 * NB), ("ffn2", 2 * FT + 4 * NB), ("odd", 4 * NB),
                        ("odd_out", NB), ("ffn3", 2 * FT + 4 * NB)):
        assert units % RING == 0
        start[name] = rounds
        rounds += units // RING
    FFNS = ((ffn1_w_gate, ffn1_w_up, ffn1_w_down, 0, 1), (ffn2_w_gate, ffn2_w_up, ffn2_w_down, 0, 3),
            (ffn1_w_gate, ffn1_w_up, ffn1_w_down, 1, 4), (ffn2_w_gate, ffn2_w_up, ffn2_w_down, 1, 6))

    with ExitStack() as ctx:
        def sb(name, shape, dt=F32):
            return ctx.enter_context(nc.sbuf_tensor(name, shape, dt))

        def sem(name):
            return ctx.enter_context(nc.semaphore(name))

        with nc.sbuf_tensor("x_tok", [P, TB, D], F32) as x_tok:
            pass
        with nc.sbuf_tensor("sq_qk", [P, 2, T], F32) as sq_qk:
            pass
        h = sb("h", [P, FT, 2, T], F32R)
        x = sb("x", [P, NB, T])
        gx = sb("gx", [P, NB, 2, T], F32R)
        raw = sb("raw", [P, RING, UNIT])
        whi = sb("whi", [P, RING, UNIT], F32R)
        wlo = sb("wlo", [P, RING, UNIT], F32R)
        R = sb("R", [P, T])
        acc = sb("acc", [P, T])
        gbuf = sb("gbuf", [P, PAD + T])
        zbuf = sb("zbuf", [P, PAD + T])
        ubuf = sb("ubuf", [P, T])
        sqbuf = sb("sqbuf", [P, T])
        obuf = sb("obuf", [P, T])
        probs = sb("probs", [P, 2, 2, T])
        ident = sb("ident", [P, P])
        ones = sb("ones", [P, P])
        mask = sb("mask", [P, P])
        halves = sb("halves", [P, 2])
        rows = sb("rows", [N_COLS, P])
        cols = sb("cols", [P, N_COLS])
        counts = sb("counts", [P, 16])
        ms = sb("ms", [P, TB, 4])
        sd = sb("sd", [P, TB, 4])
        rs = sb("rs", [P, TB, 4])
        nt = sb("nt", [P, TB, 4])
        Rc = sb("Rc", [P, TB])
        Rc2 = sb("Rc2", [P, TB])
        qscale = sb("qscale", [P, TB, 2])
        nqscale = sb("nqscale", [P, TB, 2])
        mx = sb("mx", [P, 2, 2])
        nbias = sb("nbias", [P, 2, 2])
        sums = sb("sums", [P, 2, 2])
        rec = sb("rec", [P, 2, 2])
        lam_rows = sb("lam_rows", [P, 4, HD])
        lam_prod = sb("lam_prod", [P, 2, HD])
        lam_sum = sb("lam_sum", [P, 2])
        lam_exp = sb("lam_exp", [P, 2])
        lam_pair = sb("lam_pair", [P, 2])
        sub_gain = sb("sub_gain", [P, 1])
        ps = ctx.enter_context(nc.psum_tensor("ps", [P, 8, T], F32))

        raw_in = [sem(f"raw_in{i}") for i in range(RING)]
        x_loaded = [sem(f"x_loaded{i}") for i in range(TB)]
        stored = [sem(f"stored{i}") for i in range(2)]
        (first_gains_in, params_in, lam_in, wpool_in, consts, cols_ps, cols_ready, lam_sum_ready, lam_exp_ready,
         hi_done, lo_done, w_used, xT_ps, x_new, xhi_done, sq_done, sq_added, gx_ready,
         norm_stats, norm_ms, norm_root, norm_diag, norm_spread, norm_ready,
         gate_scaled, up_scaled, silu_done, h_new, hhi_done, h_ready,
         v_hi, v_ready, q_hi, q_sq, q_taken, k_sq, k_taken, u_taken,
         qk_stats, qk_ms, qk_root, qk_diag, qk_spread, k_scaled, k_hi, k_ready,
         scores_ready, bias_ready, exp_done, w_ready, wt_ps, wt_hi, wt_ready,
         o_ps, o_sq, o_taken, o_stats, o_ms, o_root, o_diag, o_spread, o_scaled, y_hi, y_ready,
         wpool_hi, wpool_ready, pooled_new, pooled_hi, pooled_ready, pool_ps, pool_hi, pool_ready,
         group_taken, acc_zero, conv_step, conv_new, conv_hi, conv_ready, fin_ready, outT_ps, outT_copied, step) = [
            sem(name) for name in (
                "first_gains_in params_in lam_in wpool_in consts cols_ps cols_ready lam_sum_ready lam_exp_ready "
                "hi_done lo_done w_used xT_ps x_new xhi_done sq_done sq_added gx_ready "
                "norm_stats norm_ms norm_root norm_diag norm_spread norm_ready "
                "gate_scaled up_scaled silu_done h_new hhi_done h_ready "
                "v_hi v_ready q_hi q_sq q_taken k_sq k_taken u_taken "
                "qk_stats qk_ms qk_root qk_diag qk_spread k_scaled k_hi k_ready "
                "scores_ready bias_ready exp_done w_ready wt_ps wt_hi wt_ready "
                "o_ps o_sq o_taken o_stats o_ms o_root o_diag o_spread o_scaled y_hi y_ready "
                "wpool_hi wpool_ready pooled_new pooled_hi pooled_ready pool_ps pool_hi pool_ready "
                "group_taken acc_zero conv_step conv_new conv_hi conv_ready fin_ready outT_ps outT_copied step").split()]
        FIRST_SPLITS = ((), (0,), (1,), (2,), (), (3,), (), ())
        N_CONSTS = 11
        N_PARAMS = 10

        def loaded(rnd, phase):
            if phase == "odd":
                return 32 * (rnd + 1) + -16 * start["odd"]
            return 16 * (rnd + 1) + (16 * NB if phase in ("odd_out", "ffn3") else 0)

        def units_used(rnd, slot):
            return RING * rnd + slot + 1

        def spread_cols(src):
            return src.unsqueeze(2).to_broadcast([P, TB, P])

        def first_squares(m):
            return (sqbuf, obuf)[m % 2]

        def fin(s):
            return (sqbuf, obuf)[s]

        def pooled(g):
            return (gbuf, zbuf)[g % 2][:, PAD:]

        block = ctx.enter_context(nc.Block())

        @block.sync
        def _(sp):
            def load(rnd, slot, *parts, first=False):
                if not first:
                    sp.wait_ge(lo_done, RING * (rnd - 1) + slot + 1)
                at = 0
                for src in parts:
                    _, blocks, n = src.shape
                    sp.dma_start(raw[:, slot, at:at + blocks * n].rearrange("p (a n) -> p a n", a=blocks),
                                 src).then_inc(raw_in[slot], 16)
                    at += blocks * n

            def columns(w, col, first_block=0, blocks=NB, width=P):
                return w.rearrange("(c p) n -> p c n", p=P)[:, first_block:first_block + blocks,
                                                            bass.ds(col, width)]

            def row_load(row, src, loads):
                sp.dma_start(rows[row:row + src.shape[0], :], src).then_inc(loads, 16)

            def parameters():
                for r, src in ((1, mix_norm[0]), (2, ffn2_norm[0]), (3, ffn1_norm[1]), (4, mix_norm[1]),
                               (5, ffn2_norm[1])):
                    row_load(NB * r, src.rearrange("(c p) -> c p", p=P), params_in)
                row_load(COL_CONV, conv_w[0].rearrange("j (c p) -> (j c) p", p=P), params_in)
                row_load(COL_PSCALE, pool_scale[0].rearrange("(c p) -> c p", p=P), params_in)
                for row, src in ((COL_QGAIN, q_gain), (COL_KGAIN, k_gain)):
                    sp.dma_start(rows[row:row + 1, :].rearrange("a (c p) -> a c p", c=2),
                                 src.unsqueeze(1).to_broadcast([1, 2, HD])).then_inc(params_in, 16)
                row_load(COL_SUB, subln_gain, params_in)
                for j, src in enumerate((lambda_q1, lambda_q2, lambda_k1, lambda_k2)):
                    sp.dma_start(lam_rows[:, j, :], src.to_broadcast([P, HD])).then_inc(lam_in, 16)

            def ffn(f):
                w_gate, w_up, w_down, layer, _ = FFNS[f]
                r0 = start[f"ffn{f}"]
                r1 = r0 + FT // 2

                def two_tiles(i, first=False):
                    for s in range(2):
                        load(r0 + i, 2 * s, columns(w_gate[layer], (2 * i + s) * P), first=first)
                        load(r0 + i, 2 * s + 1, columns(w_up[layer], (2 * i + s) * P), first=first)

                if f == 0:
                    two_tiles(0, first=True)
                    parameters()
                with sp.Fori(1 if f == 0 else 0, FT // 2) as i:
                    two_tiles(i)
                with sp.Fori(0, NB) as m:
                    for s in range(RING):
                        load(r1 + m, s, columns(w_down[layer], m * P, DOWN_FIRST[s], DOWN_UNITS[s]))

            def out_projection(name, w):
                with sp.Fori(0, NB // RING) as i:
                    for s in range(RING):
                        load(start[name] + i, s, columns(w, (RING * i + s) * P))

            row_load(0, ffn1_norm[0].rearrange("(c p) -> c p", p=P), first_gains_in)
            for tb in range(TB):
                sp.dma_start(x_tok[:, tb, :], x_in[0, tb * P:(tb + 1) * P, :]).then_inc(x_loaded[tb], 16)
            ffn(0)
            r0 = start["even"]
            for s in range(RING):
                load(r0, s, columns(even_w_in[0], 2 * T, 2 * s, 2, T))
            for n in range(3 * HEADS):
                head, kind = divmod(n, 3)
                load(r0 + 1 + n // RING, n % RING, columns(even_w_in[0], (0, T, 3 * T)[kind] + head * P))
                if n == 2:
                    sp.wait_ge(norm_ms, 2)
                    sp.dma_start(acc[:, :].rearrange("p (g d) -> p g d", g=HEADS),
                                 w_pool[0].rearrange("g c d -> c g d")).then_inc(wpool_in, 16)
            out_projection("even_out", even_w_out[0])
            ffn(1)
            ffn(2)
            w_bch = odd_w_in[0].rearrange("(c p) (k n) -> p c k n", p=P, k=3)
            with sp.Fori(0, NB) as g:
                for s in range(RING):
                    load(start["odd"] + g, s, *(w_bch[:, 2 * s + j, :, bass.ds(g * P, P)] for j in range(2)))
            out_projection("odd_out", odd_w_out[0])
            ffn(3)
            for s in range(2):
                sp.wait_ge(stored[s], 16 * (NB // 2))

        @block.gpsimd
        def _(pool):
            pool.memset(ones[:, :], 1.0).then_inc(consts, 1)
            pool.memset(ident[:, :], 0.0).then_inc(consts, 1)
            pool.memset(mask[:, :], 0.0).then_inc(consts, 1)
            pool.memset(halves[:, :], 0.0).then_inc(consts, 1)
            pool.memset(gbuf[:, 0:PAD], 0.0).then_inc(consts, 1)
            pool.memset(zbuf[:, 0:PAD], 0.0).then_inc(consts, 1)
            pool.wait_ge(consts, 6)
            pool.affine_select(out=ident[:, :], in_=ident[:, :], compare_op=ALU.not_equal, fill=1.0,
                               base=0, pattern=[[-1, P]], channel_multiplier=1).then_inc(consts, 1)
            pool.affine_select(out=mask[:, :], in_=mask[:, :], compare_op=ALU.is_ge, fill=MASKED,
                               base=0, pattern=[[-1, P]], channel_multiplier=1).then_inc(consts, 1)
            pool.wait_ge(consts, 8)
            pool.memset(halves[0:HD, 0:1], 1.0).then_inc(consts, 1)
            pool.wait_ge(consts, 9)
            pool.memset(halves[HD:P, 1:2], 1.0).then_inc(consts, 1)
            pool.wait_ge(consts, 10)
            for t in range(max(WINDOWS)):
                last = pool.memset(counts[:, t:t + 1], 1.0 / (t + 1))
            last.then_inc(consts, 1)
            pool.memset(acc[:, :], 0.0).then_inc(acc_zero, 1)
            pool.wait_ge(acc_zero, 1)
            for m in range(NB):
                pool.wait_ge(sq_done, m + 1)
                pool.tensor_tensor(acc[:, :], acc[:, :], first_squares(m)[:, :], ALU.add).then_inc(sq_added, 1)
                pool.wait_ge(sq_added, m + 1)

        @block.tensor
        def _(pe):
            def product(dst, lhs, rhs, begin, end):
                pe.matmul(dst, lhs[0], rhs[0], start=begin, stop=False)
                pe.matmul(dst, lhs[0], rhs[1], start=False, stop=False)
                return pe.matmul(dst, lhs[1], rhs[0], start=False, stop=end)

            def weight(slot, i, n=P):
                return whi[:, slot, i * n:(i + 1) * n], wlo[:, slot, i * n:(i + 1) * n]

            def gxb(k, a=0, b=T):
                return gx[:, k, 0, a:b], gx[:, k, 1, a:b]

            def hb(k, a=0, b=T, p0=0, p1=P):
                return h[p0:p1, k, 0, a:b], h[p0:p1, k, 1, a:b]

            def column_block(rnd, slot, bank, norm=None):
                pe.wait_ge(lo_done, RING * rnd + slot + 1)
                for k in range(NB):
                    if norm is not None:
                        pe.wait_ge(gx_ready, NB * norm + k + 1)
                    last = product(ps[:, bank, :], weight(slot, k), gxb(k), k == 0, k == NB - 1)
                last.then_inc(w_used, 1)

            def stats_of_norm(r):
                pe.wait_ge(sq_added, NB * (r + 1))
                for tb in range(TB):
                    last = pe.matmul(ps[:, STAT_BANK, tb:tb + 1], acc[:, tb * P:(tb + 1) * P], ones[:, 0:1],
                                     start=True, stop=True)
                last.then_inc(norm_stats, 1)

            def spread_of_norm(r):
                pe.wait_ge(norm_diag, r + 1)
                pe.matmul(ps[:, SPREAD_BANK, :], ones[:, :], obuf[:, :], start=True,
                          stop=True).then_inc(norm_spread, 1)

            def transpose_result(m, s, first=False):
                pe.wait_ge(fin_ready, m + 1)
                if not first:
                    pe.wait_ge(outT_copied, m - 1)
                for tb in range(TB):
                    last = pe.transpose(ps[:, OUT_BANKS[s], tb * P:(tb + 1) * P],
                                        fin(s)[:, tb * P:(tb + 1) * P], ident[:, :])
                last.then_inc(outT_ps, 1)

            def ffn(f):
                phase = FFNS[f][4]
                r0 = start[f"ffn{f}"]
                r1 = r0 + FT // 2

                def two_tiles(i, first=False):
                    for s in range(2):
                        new = first and s == 0
                        if not first:
                            pe.wait_ge(up_scaled, FT * f + 2 * i + s - 1)
                        column_block(r0 + i, 2 * s, GATE_BANKS[s], phase - 1 if new else None)
                        if new:
                            stats_of_norm(phase - 1)
                        column_block(r0 + i, 2 * s + 1, GATE_BANKS[s] + 1)
                        if new:
                            spread_of_norm(phase - 1)

                def first_tiles():
                    for part in range(2):
                        for n in range(RING):
                            if part == 0:
                                pe.wait_ge(lo_done, n + 1)
                            for k in range(part * NB // 2, (part + 1) * NB // 2):
                                if n == 0:
                                    pe.wait_ge(gx_ready, k + 1)
                                last = product(ps[:, n, :], weight(n, k), gxb(k), k == 0, k == NB - 1)
                            if part == 1:
                                last.then_inc(w_used, 1)
                            if part == 1 and n == 0:
                                pe.wait_ge(consts, N_CONSTS)
                                pe.wait_ge(params_in, 16 * N_PARAMS)
                                pe.transpose(ps[:, SPREAD_BANK, 0:N_COLS], rows[:, :],
                                             ident[0:N_COLS, 0:N_COLS]).then_inc(cols_ps, 1)
                                stats_of_norm(0)
                            if part == 1 and n == 1:
                                pe.wait_ge(cols_ready, 2)
                                spread_of_norm(0)

                def down_tile(m, s, first=False):
                    for q in range(RING):
                        pe.wait_ge(lo_done, RING * (r1 + m) + q + 1)
                        for j in range(DOWN_UNITS[q]):
                            k = DOWN_FIRST[q] + j
                            if first and k == FT - 1:
                                pe.wait_ge(h_ready, FT * (f + 1))
                            last = product(ps[:, RES_BANKS[s], :], weight(q, j), hb(k), k == 0, k == FT - 1)
                        last.then_inc(w_used, 1)

                if f == 0:
                    first_tiles()
                else:
                    two_tiles(0, first=True)
                with pe.Fori(1, FT // 2) as i:
                    two_tiles(i)
                pe.wait_ge(h_ready, FT * (f + 1) - 1)
                if f < 3:
                    pe.wait_ge(x_new, NB * phase - 1)
                    down_tile(0, 0, first=True)
                    pe.wait_ge(x_new, NB * phase)
                    down_tile(1, 1)
                    with pe.Fori(1, NB // 2) as i:
                        for s in range(2):
                            m = 2 * i + s
                            pe.wait_ge(x_new, NB * phase + m - 1)
                            down_tile(m, s)
                else:
                    down_tile(0, 0, first=True)
                    down_tile(1, 1)
                    for s in range(2):
                        transpose_result(s, s, first=True)
                        down_tile(2 + s, s)
                    with pe.Fori(2, NB // 2) as i:
                        for s in range(2):
                            m = 2 * i + s
                            transpose_result(m - 2, s)
                            down_tile(m, s)
                    transpose_result(NB - 2, 0)
                    transpose_result(NB - 1, 1)

            def out_projection(name, phase, blocks, last_ready, count):
                r0 = start[name]

                def part(m, js):
                    for j in js:
                        last = product(ps[:, RES_BANKS[m % 2], :], weight(m % RING, blocks[j]),
                                       hb(Y0 + blocks[j]), j == 0, j == NB - 1)
                    return last

                for m in range(NB):
                    pe.wait_ge(x_new, NB * phase + m - 1)
                    pe.wait_ge(lo_done, RING * r0 + m + 1)
                    if m < 2:
                        part(m, range(NB - 1))
                    else:
                        part(m, range(NB)).then_inc(w_used, 1)
                    if m == 1:
                        pe.wait_ge(last_ready, count)
                        part(0, [NB - 1]).then_inc(w_used, 1)
                        part(1, [NB - 1]).then_inc(w_used, 1)

            def scores(hd, qb):
                if 4 * hd + qb >= 2:
                    pe.wait_ge(exp_done, 4 * hd + qb - 1)
                for c in range(2):
                    p0, p1 = c * HD, (c + 1) * HD
                    last = product(ps[:, SCORE_BANKS[qb % 2] + c, 0:(qb + 1) * P],
                                   hb(Q0 + hd % 2, qb * P, (qb + 1) * P, p0, p1),
                                   hb(K0, 0, (qb + 1) * P, p0, p1), True, True)
                last.then_inc(scores_ready, 1)

            def transpose_weights(hd, qb):
                pe.wait_ge(w_ready, 4 * hd + qb + 1)
                if 4 * hd + qb:
                    pe.wait_ge(wt_ready, 4 * hd + qb)
                for kb in range(qb + 1):
                    last = pe.transpose(ps[:, STAT_BANK, kb * P:(kb + 1) * P],
                                        probs[:, qb % 2, 0, kb * P:(kb + 1) * P], ident[:, :])
                last.then_inc(wt_ps, 1)

            def even_mixer():
                r0 = start["even"]
                for s in range(RING):
                    pe.wait_ge(lo_done, RING * r0 + s + 1)
                    for j in range(2):
                        k = 2 * s + j
                        pe.wait_ge(gx_ready, NB + k + 1)
                        for tb in range(TB):
                            if k == 0 and V_BANK + tb in RES_BANKS:
                                pe.wait_ge(x_new, 2 * NB + V_BANK + tb - RES_BANKS[1])
                            last = product(ps[:, V_BANK + tb, :], gxb(k, tb * P, (tb + 1) * P),
                                           weight(s, j, T), k == 0, k == NB - 1)
                    last.then_inc(w_used, 1)
                stats_of_norm(1)

                def unit_of(n):
                    return r0 + 1 + n // RING, n % RING

                for st in range(HEADS + 2):
                    cur, prev, older = st, st - 1, st - 2
                    if cur < HEADS:
                        if cur:
                            pe.wait_ge(u_taken, cur)
                        column_block(*unit_of(3 * cur), Q_BANK)
                    if cur == 0:
                        spread_of_norm(1)
                    if 0 <= older < HEADS:
                        pe.wait_ge(o_sq, older + 1)
                        if prev < HEADS:
                            pe.wait_ge(qk_ms, prev + 1)
                        else:
                            pe.wait_ge(wt_ready, 4 * HEADS)
                        for tb in range(TB):
                            last = pe.matmul(ps[:, STAT_BANK, tb:tb + 1], sqbuf[:, tb * P:(tb + 1) * P],
                                             ones[:, 0:1], start=True, stop=True)
                        last.then_inc(o_stats, 1)
                    if 0 <= prev < HEADS:
                        pe.wait_ge(wpool_ready, 1)
                        pe.wait_ge(pooled_ready, prev + 1)
                        last = product(ps[:, POOL_BANK, :], hb(WPOOL, prev * P, (prev + 1) * P), hb(POOLED),
                                       True, True)
                        last.then_inc(pool_ps, 1)
                        pe.wait_ge(qk_diag, prev + 1)
                        if prev:
                            pe.wait_ge(o_taken, prev)
                        else:
                            pe.wait_ge(norm_ready, 2)
                        for c in range(2):
                            last = pe.matmul(ps[c * HD:(c + 1) * HD, SPREAD_BANK, :], ones[:, 0:HD],
                                             sq_qk[:, c, :], start=True, stop=True)
                        last.then_inc(qk_spread, 1)
                        pe.wait_ge(v_ready, TB)
                        pe.wait_ge(q_taken, prev + 1)
                        pe.wait_ge(k_ready, prev + 1)
                        scores(prev, 0)
                        scores(prev, 1)
                    if cur < HEADS:
                        if cur:
                            pe.wait_ge(pool_ready, cur)
                        column_block(*unit_of(3 * cur + 1), K_BANK)
                    if 0 <= prev < HEADS:
                        if older >= 0:
                            pe.wait_ge(o_ms, older + 1)
                        else:
                            pe.wait_ge(qk_ms, prev + 1)
                        transpose_weights(prev, 0)
                        scores(prev, 2)
                        transpose_weights(prev, 1)
                        scores(prev, 3)
                    if 0 <= older < HEADS:
                        pe.wait_ge(o_diag, older + 1)
                        if prev < HEADS:
                            pe.wait_ge(k_scaled, prev + 1)
                        else:
                            pe.wait_ge(o_taken, HEADS)
                        pe.matmul(ps[:, SPREAD_BANK, :], ones[:, :], obuf[:, :], start=True,
                                  stop=True).then_inc(o_spread, 1)
                    if cur < HEADS:
                        pe.wait_ge(q_taken, cur + 1)
                        pe.wait_ge(q_sq, cur + 1)
                        column_block(*unit_of(3 * cur + 2), U_BANK)
                    if 0 <= prev < HEADS:
                        transpose_weights(prev, 2)
                        transpose_weights(prev, 3)
                        pe.wait_ge(wt_ready, 4 * (prev + 1))
                        if older >= 0:
                            pe.wait_ge(o_scaled, older + 1)
                        for kb in range(TB):
                            last = product(ps[:, SPREAD_BANK, kb * P:T], hb(V0 + kb, prev * P, (prev + 1) * P),
                                           hb(WT0 + kb, kb * P, T), kb == 0, kb == TB - 1)
                        last.then_inc(o_ps, 1)
                    if cur < HEADS:
                        pe.wait_ge(k_sq, cur + 1)
                        if prev < 0:
                            pe.wait_ge(norm_ready, 2)
                        for j in range(2):
                            for tb in range(TB):
                                last = pe.matmul(ps[:, STAT_BANK, 4 * tb + 2 * j:4 * tb + 2 * j + 2],
                                                 sq_qk[:, j, tb * P:(tb + 1) * P], halves[:, :],
                                                 start=True, stop=True)
                        last.then_inc(qk_stats, 1)
                pe.wait_ge(pool_ready, HEADS)
                pe.wait_ge(y_ready, HEADS - 1)
                out_projection("even_out", 2, [*range(HEADS, NB), *range(HEADS)], y_ready, HEADS)

            def odd_mixer():
                r0 = start["odd"]

                def two_groups(i, first=False):
                    for s in range(2):
                        if not first:
                            pe.wait_ge(group_taken, 2 * i + s - 1)
                        if first and s == 1:
                            pe.wait_ge(norm_ready, 5)
                        for q in range(RING):
                            pe.wait_ge(lo_done, RING * (r0 + 2 * i + s) + q + 1)
                            for j in range(2):
                                k = 2 * q + j
                                if first and s == 0:
                                    pe.wait_ge(gx_ready, 4 * NB + k + 1)
                                for kind in range(3):
                                    last = product(ps[:, GROUP_BANKS[s][kind], :], weight(q, 3 * j + kind), gxb(k),
                                                   k == 0, k == NB - 1)
                            last.then_inc(w_used, 1)
                            if first and s == 0 and q == 1:
                                stats_of_norm(4)
                        if first and s == 0:
                            spread_of_norm(4)

                two_groups(0, True)
                with pe.Fori(1, NB // 2) as i:
                    two_groups(i)
                pe.wait_ge(conv_ready, NB - 1)
                out_projection("odd_out", 5, range(NB), conv_ready, NB)

            pe.wait_ge(consts, 8)
            pe.wait_ge(first_gains_in, 16)
            pe.transpose(ps[:, SPREAD_BANK, 0:NB], rows[0:NB, :], ident[0:NB, 0:NB]).then_inc(cols_ps, 1)
            for tb in range(TB):
                pe.wait_ge(x_loaded[tb], 16)
                for m in range(NB):
                    if tb == 0 and m == SPREAD_BANK:
                        pe.wait_ge(cols_ready, 1)
                    tile = pe.transpose(ps[:, m, tb * P:(tb + 1) * P], x_tok[:, tb, m * P:(m + 1) * P],
                                        ident[:, :])
                    if tb == TB - 1:
                        tile.then_inc(xT_ps, 1)
            ffn(0)
            even_mixer()
            ffn(1)
            ffn(2)
            odd_mixer()
            ffn(3)

        @block.scalar
        def _(act):
            def round_unit(rnd, slot, blocks=NB, first=False, phase=None):
                act.wait_ge(raw_in[slot], loaded(rnd, phase))
                if not first:
                    act.wait_ge(w_used, units_used(rnd - 1, slot))
                act.activation(whi[:, slot, 0:blocks * P], raw[:, slot, 0:blocks * P],
                               ACT.Copy).then_inc(hi_done, 1)

            def residual(phase, m):
                g = NB * phase + m
                act.wait_ge(cols_ready, 2)
                act.wait_ge(x_new, g + 1)
                act.activation(gx[:, m, 0, :], x[:, m, :], ACT.Copy,
                               scale=cols[:, bass.ds(g, 1)]).then_inc(xhi_done, 1)
                act.wait_ge(cols_ready, 2)
                act.wait_ge(sq_added, g)
                act.activation(sqbuf[:, :], x[:, m, :], ACT.Square).then_inc(sq_done, 1)

            def root(ms_ready, count, n, done):
                act.wait_ge(ms_ready, count)
                act.activation(sd[:, :, 0:n], ms[:, :, 0:n], ACT.Sqrt).then_inc(done, 1)

            def ffn(f):
                phase = FFNS[f][4]
                r0 = start[f"ffn{f}"]
                r1 = r0 + FT // 2

                def activate(t):
                    act.wait_ge(gate_scaled, FT * f + t + 1)
                    act.activation(gbuf[:, PAD:], gbuf[:, PAD:], ACT.Silu).then_inc(silu_done, 1)
                    act.wait_ge(cols_ready, 1)
                    act.wait_ge(h_new, FT * f + t + 1)
                    act.activation(h[:, t, 0, :], ubuf[:, :], ACT.Copy).then_inc(hhi_done, 1)

                name = f"ffn{f}"

                def two_tiles(i, first=False):
                    if not first:
                        round_unit(r0 + i, 2, phase=name)
                        round_unit(r0 + i, 3, phase=name)
                    activate(2 * i)
                    round_unit(r0 + i + 1, 0, phase=name)
                    round_unit(r0 + i + 1, 1, phase=name)
                    activate(2 * i + 1)

                root(norm_ms, phase, 1, norm_root)
                two_tiles(0, first=f == 0)
                if f == 0:
                    act.wait_ge(lam_sum_ready, 1)
                    act.activation(lam_exp[:, :], lam_sum[:, :], ACT.Exp).then_inc(lam_exp_ready, 1)
                with act.Fori(1, FT // 2 - 1) as i:
                    two_tiles(i)
                round_unit(r1 - 1, 2, phase=name)
                round_unit(r1 - 1, 3, phase=name)
                activate(FT - 2)
                for s in range(RING):
                    round_unit(r1, s, DOWN_UNITS[s], phase=name)
                activate(FT - 1)

                def next_tile(m):
                    for s in range(RING):
                        round_unit(r1 + m + 1, s, DOWN_UNITS[s], phase=name)

                if f < 3:
                    with act.Fori(0, NB - 1) as m:
                        next_tile(m)
                        residual(phase, m)
                else:
                    next_tile(0)
                    for s in range(2):
                        next_tile(s + 1)
                        store_result(s, s, first=True)
                    with act.Fori(1, NB // 2 - 1) as i:
                        for s in range(2):
                            next_tile(2 * i + s + 1)
                            store_result(2 * i + s, s)
                    store_result(NB - 2, 0)
                    store_result(NB - 1, 1)
                if f < 3:
                    blocks = 6 if f == 2 else NB
                    after = "odd" if f == 2 else None
                    round_unit(r1 + NB, 0, blocks, phase=after)
                    round_unit(r1 + NB, 1, blocks, phase=after)
                    residual(phase, NB - 1)

            def out_projection(name, phase):
                with act.Fori(0, NB // RING) as i:
                    for s in range(RING):
                        round_unit(start[name] + i + (s + 2) // RING, (s + 2) % RING, phase=name)
                        residual(phase, RING * i + s)

            def store_result(m, s, first=False):
                act.wait_ge(outT_ps, m + 1)
                if not first:
                    act.wait_ge(stored[s], 8 * m - 8 * s)
                act.activation(probs[:, s, 0, :], ps[:, OUT_BANKS[s], :], ACT.Copy).then_inc(outT_copied, 1)
                act.wait_ge(outT_copied, m + 1)
                act.dma_start(out[0].rearrange("(b p) d -> p b d", p=P)[:, :, bass.ds(m * P, P)],
                              probs[:, s, 0, :].rearrange("p (b n) -> p b n", b=TB)).then_inc(stored[s], 16)

            def exps(hd, qb):
                act.wait_ge(bias_ready, 4 * hd + qb + 1)
                if 4 * hd + qb >= 2:
                    act.wait_ge(wt_ps, 4 * hd + qb - 1)
                for c in range(2):
                    last = act.activation(probs[:, qb % 2, c, 0:(qb + 1) * P],
                                          ps[:, SCORE_BANKS[qb % 2] + c, 0:(qb + 1) * P], ACT.Exp,
                                          scale=qscale[:, qb, c:c + 1], bias=nbias[:, qb % 2, c:c + 1],
                                          accum_out=sums[:, qb % 2, c:c + 1])
                last.then_inc(exp_done, 1)

            def round_weights(hd, qb):
                act.wait_ge(wt_ps, 4 * hd + qb + 1)
                if qb == 0 and hd:
                    act.wait_ge(o_ps, hd)
                act.activation(h[:, WT0:WT0 + qb + 1, 0, qb * P:(qb + 1) * P],
                               ps[:, STAT_BANK, 0:(qb + 1) * P].rearrange("p (k n) -> p k n", n=P),
                               ACT.Copy).then_inc(wt_hi, 1)

            def even_mixer():
                r0 = start["even"]

                def round_ahead(n):
                    round_unit(r0 + 1 + (n + 2) // RING, (n + 2) % RING)

                round_unit(r0, 2)
                round_unit(r0, 3)
                round_unit(r0 + 1, 0)
                round_unit(r0 + 1, 1)
                root(norm_ms, 2, 1, norm_root)
                act.wait_ge(norm_ready, 2)
                for tb in range(TB):
                    act.activation(h[:, V0 + tb, 0, :], ps[:, V_BANK + tb, :], ACT.Copy,
                                   scale=Rc[:, tb:tb + 1]).then_inc(v_hi, 1)
                for st in range(HEADS + 2):
                    cur, prev, older = st, st - 1, st - 2
                    if cur < HEADS:
                        round_ahead(3 * cur)
                        act.wait_ge(w_used, units_used(r0 + 1, 3 * cur))
                        act.activation(h[:, Q0 + cur % 2, 0, :], ps[:, Q_BANK, :], ACT.Copy,
                                       scale=cols[:, COL_QGAIN:COL_QGAIN + 1]).then_inc(q_hi, 1)
                    if cur == 0:
                        act.wait_ge(wpool_in, 16)
                        act.activation(h[:, WPOOL, 0, :], acc[:, :], ACT.Copy).then_inc(wpool_hi, 1)
                    if 0 <= older < HEADS:
                        root(o_ms, older + 1, 1, o_root)
                    if 0 <= prev < HEADS:
                        act.wait_ge(pool_ps, prev + 1)
                        act.activation(h[:, Y0 + HEADS + prev, 0, :], ps[:, POOL_BANK, :], ACT.Copy,
                                       scale=cols[:, COL_PSCALE + prev:COL_PSCALE + prev + 1]).then_inc(pool_hi, 1)
                        act.wait_ge(qk_spread, prev + 1)
                    if cur < HEADS:
                        act.wait_ge(q_taken, cur + 1)
                        act.activation(sq_qk[:, 0, :], ps[:, Q_BANK, :], ACT.Square).then_inc(q_sq, 1)
                    if 0 <= prev < HEADS:
                        act.wait_ge(k_scaled, prev + 1)
                        act.activation(h[:, K0, 0, :], ubuf[:, :], ACT.Copy).then_inc(k_hi, 1)
                        exps(prev, 0)
                        exps(prev, 1)
                    if cur < HEADS:
                        round_ahead(3 * cur + 1)
                        act.wait_ge(k_taken, cur + 1)
                        act.activation(sq_qk[:, 1, :], ps[:, K_BANK, :], ACT.Square).then_inc(k_sq, 1)
                    if 0 <= prev < HEADS:
                        round_weights(prev, 0)
                        exps(prev, 2)
                        round_weights(prev, 1)
                        exps(prev, 3)
                    if 0 <= older < HEADS:
                        act.wait_ge(o_scaled, older + 1)
                        act.activation(h[:, Y0 + older, 0, :], acc[:, :], ACT.Copy).then_inc(y_hi, 1)
                    if cur < HEADS:
                        round_ahead(3 * cur + 2)
                    if 0 <= prev < HEADS:
                        round_weights(prev, 2)
                        round_weights(prev, 3)
                        act.wait_ge(o_ps, prev + 1)
                        act.activation(sqbuf[:, :], ps[:, SPREAD_BANK, :], ACT.Square).then_inc(o_sq, 1)
                    if cur < HEADS:
                        root(qk_ms, cur + 1, 4, qk_root)
                        act.wait_ge(pooled_new, cur + 1)
                        act.activation(h[:, POOLED, 0, :], pooled(cur), ACT.Copy).then_inc(pooled_hi, 1)
                out_projection("even_out", 2)

            def odd_mixer():
                r0 = start["odd"]

                def group(g, next_blocks=6, stats=False, following="odd"):
                    if stats:
                        round_unit(r0, 2, 6, phase="odd")
                        round_unit(r0, 3, 6, phase="odd")
                        root(norm_ms, 5, 1, norm_root)
                    for slot in range(RING if following == "odd" else 2):
                        round_unit(r0 + g + 1, slot, next_blocks, phase=following)
                    act.wait_ge(cols_ready, 1)
                    act.wait_ge(conv_new, g + 1)
                    act.activation(h[:, Y0 + g, 0, :], obuf[:, :], ACT.Copy).then_inc(conv_hi, 1)

                group(0, stats=True)
                with act.Fori(1, NB - 1) as g:
                    group(g)
                group(NB - 1, next_blocks=NB, following="odd_out")
                out_projection("odd_out", 5)

            act.wait_ge(cols_ready, 1)
            for m in range(NB):
                act.wait_ge(x_new, m + 1)
                act.activation(gx[:, m, 0, :], x[:, m, :], ACT.Copy, scale=cols[:, m:m + 1]).then_inc(xhi_done, 1)
                for slot in FIRST_SPLITS[m]:
                    round_unit(0, slot, first=True)
                if m >= 2:
                    act.wait_ge(sq_added, m - 1)
                act.activation(first_squares(m)[:, :], x[:, m, :], ACT.Square).then_inc(sq_done, 1)
            ffn(0)
            even_mixer()
            ffn(1)
            ffn(2)
            odd_mixer()
            ffn(3)

        @block.vector
        def _(dve):
            steps = [0]

            def then(instruction):
                steps[0] += 1
                instruction.then_inc(step, 1)
                dve.wait_ge(step, steps[0])

            def split_unit(rnd, slot, blocks=NB):
                dve.wait_ge(hi_done, RING * rnd + slot + 1)
                dve.tensor_tensor(wlo[:, slot, 0:blocks * P], raw[:, slot, 0:blocks * P],
                                  whi[:, slot, 0:blocks * P], ALU.subtract).then_inc(lo_done, 1)

            def rest_of_gx(phase, m):
                g = NB * phase + m
                dve.wait_ge(xhi_done, g + 1)
                dve.wait_ge(x_new, g + 1)
                dve.scalar_tensor_tensor(gx[:, m, 1, :], x[:, m, :], cols[:, bass.ds(g, 1)],
                                         gx[:, m, 0, :], ALU.mult, ALU.subtract).then_inc(gx_ready, 1)

            def residual(phase, m, bank, coefficient, ready, count):
                g = NB * phase + m
                dve.wait_ge(ready, count)
                dve.scalar_tensor_tensor(x[:, m, :], ps[:, bank, :], coefficient, x[:, m, :],
                                         ALU.mult, ALU.add).then_inc(x_new, 1)
                rest_of_gx(phase, m)
                dve.wait_ge(sq_done, g + 1)
                dve.wait_ge(sq_added, g)
                dve.tensor_tensor(acc[:, :], acc[:, :], sqbuf[:, :], ALU.add).then_inc(sq_added, 1)

            def clear_acc():
                then(dve.memset(acc[:, :], 0.0))

            def inverse_root(n, ms_done, root_done, count):
                a, b, c, d = rs[:, :, 0:n], nt[:, :, 0:n], ms[:, :, 0:n], sd[:, :, 0:n]
                dve.wait_ge(ms_done, count)
                dve.wait_ge(root_done, count)
                then(dve.reciprocal(a, d))
                then(dve.tensor_tensor(b, a, a, ALU.mult))
                then(dve.tensor_tensor(b, b, c, ALU.mult))
                then(dve.tensor_scalar(b, b, -0.5, 1.5, ALU.mult, ALU.add))
                then(dve.tensor_tensor(a, a, b, ALU.mult))

            def diagonal(dst, factors):
                return dve.tensor_tensor(dst.rearrange("p (b n) -> p b n", b=TB),
                                         ident[:, :].unsqueeze(1).to_broadcast([P, TB, P]),
                                         factors.to_broadcast([P, TB, P]), ALU.mult)

            def norm_factors(r):
                dve.wait_ge(norm_stats, r + 1)
                dve.tensor_scalar(ms[:, :, 0:1], ps[:, STAT_BANK, 0:TB].unsqueeze(2), 1.0 / D, EPS,
                                  ALU.mult, ALU.add).then_inc(norm_ms, 1)
                inverse_root(1, norm_ms, norm_root, r + 1)
                then(dve.tensor_copy(Rc[:, :].unsqueeze(2), rs[:, :, 0:1]))
                diagonal(obuf[:, :], Rc[:, :].unsqueeze(2)).then_inc(norm_diag, 1)

            def norm_rows(r):
                dve.wait_ge(norm_spread, r + 1)
                dve.tensor_copy(R[:, :], ps[:, SPREAD_BANK, :]).then_inc(norm_ready, 1)
                dve.wait_ge(norm_ready, r + 1)

            def ffn(f):
                phase = FFNS[f][4]
                r0 = start[f"ffn{f}"]
                r1 = r0 + FT // 2

                def hidden(t, s):
                    dve.wait_ge(w_used, RING * r0 + 2 * t + 2)
                    dve.tensor_tensor(gbuf[:, PAD:], ps[:, GATE_BANKS[s], :], R[:, :],
                                      ALU.mult).then_inc(gate_scaled, 1)
                    dve.wait_ge(h_ready, FT * f + t)
                    dve.tensor_tensor(ubuf[:, :], ps[:, GATE_BANKS[s] + 1, :], R[:, :],
                                      ALU.mult).then_inc(up_scaled, 1)
                    dve.wait_ge(silu_done, FT * f + t + 1)
                    dve.wait_ge(up_scaled, FT * f + t + 1)
                    dve.tensor_tensor(ubuf[:, :], gbuf[:, PAD:], ubuf[:, :], ALU.mult).then_inc(h_new, 1)
                    dve.wait_ge(hhi_done, FT * f + t + 1)
                    dve.tensor_tensor(h[:, t, 1, :], ubuf[:, :], h[:, t, 0, :],
                                      ALU.subtract).then_inc(h_ready, 1)

                def two_tiles(i):
                    split_unit(r0 + i, 2)
                    split_unit(r0 + i, 3)
                    hidden(2 * i, 0)
                    split_unit(r0 + i + 1, 0)
                    split_unit(r0 + i + 1, 1)
                    hidden(2 * i + 1, 1)

                norm_factors(phase - 1)
                if f:
                    split_unit(r0, 2)
                    split_unit(r0, 3)
                norm_rows(phase - 1)
                hidden(0, 0)
                split_unit(r0 + 1, 0)
                split_unit(r0 + 1, 1)
                hidden(1, 1)
                if f == 0:
                    dve.wait_ge(lam_in, 4 * 16)
                    then(dve.tensor_tensor(lam_prod[:, :, :], lam_rows[:, 0:2, :], lam_rows[:, 2:4, :],
                                           ALU.mult))
                    dve.reduce_sum(lam_sum[:, :], lam_prod[:, :, :], AX_X).then_inc(lam_sum_ready, 1)
                    dve.memset(lam_pair[:, 0:1], 1.0)
                    dve.wait_ge(lam_exp_ready, 1)
                    then(dve.tensor_tensor(lam_pair[:, 1:2], lam_exp[:, 1:2], lam_exp[:, 0:1], ALU.subtract))
                    then(dve.tensor_scalar(lam_pair[:, 1:2], lam_pair[:, 1:2], -LAM_INIT, None, ALU.add))
                with dve.Fori(1, FT // 2 - 1) as i:
                    two_tiles(i)
                split_unit(r1 - 1, 2)
                split_unit(r1 - 1, 3)
                hidden(FT - 2, 0)
                for s in range(RING):
                    split_unit(r1, s, DOWN_UNITS[s])
                hidden(FT - 1, 1)
                clear_acc()

                def next_tile(m):
                    for s in range(RING):
                        split_unit(r1 + m + 1, s, DOWN_UNITS[s])

                def down_result(m, s, first=False):
                    dve.wait_ge(w_used, units_used(r1 + m, RING - 1))
                    if not first:
                        dve.wait_ge(outT_ps, m - 1)
                    dve.scalar_tensor_tensor(fin(s)[:, :], ps[:, RES_BANKS[s], :], 0.5, x[:, m, :],
                                             ALU.mult, ALU.add).then_inc(fin_ready, 1)

                def down_residual(m, s):
                    residual(phase, m, RES_BANKS[s], 0.5, w_used, units_used(r1 + m, RING - 1))

                if f < 3:
                    with dve.Fori(0, NB // 2 - 1) as i:
                        for s in range(2):
                            next_tile(2 * i + s)
                            down_residual(2 * i + s, s)
                    next_tile(NB - 2)
                    down_residual(NB - 2, 0)
                    blocks = 6 if f == 2 else NB
                    split_unit(r1 + NB, 0, blocks)
                    split_unit(r1 + NB, 1, blocks)
                    down_residual(NB - 1, 1)
                else:
                    for m in range(2):
                        next_tile(m)
                        down_result(m, m, first=True)
                    with dve.Fori(1, NB // 2 - 1) as i:
                        for s in range(2):
                            next_tile(2 * i + s)
                            down_result(2 * i + s, s)
                    next_tile(NB - 2)
                    down_result(NB - 2, 0)
                    down_result(NB - 1, 1)

            def out_projection(name, phase):
                with dve.Fori(0, NB // RING) as i:
                    for s in range(RING):
                        split_unit(start[name] + i + (s + 2) // RING, (s + 2) % RING)
                        residual(phase, RING * i + s, RES_BANKS[s % 2], 1.0, w_used,
                                 units_used(start[name] + i, s))

            def row_maxima(hd, qb):
                n = (qb + 1) * P
                pair = ps[:, SCORE_BANKS[qb % 2]:SCORE_BANKS[qb % 2] + 2, :]
                dve.wait_ge(scores_ready, 4 * hd + qb + 1)
                then(dve.tensor_tensor(pair[:, :, n - P:n], pair[:, :, n - P:n],
                                       mask[:, :].unsqueeze(1).to_broadcast([P, 2, P]), ALU.add))
                then(dve.reduce_max(mx[:, qb % 2, :], pair[:, :, 0:n], AX_X))
                dve.tensor_tensor(nbias[:, qb % 2, :], mx[:, qb % 2, :], nqscale[:, qb, :],
                                  ALU.mult).then_inc(bias_ready, 1)

            def combine(hd, qb):
                n = (qb + 1) * P
                dve.wait_ge(exp_done, 4 * hd + qb + 1)
                then(dve.reciprocal(rec[:, qb % 2, :], sums[:, qb % 2, :]))
                then(dve.tensor_tensor(rec[:, qb % 2, :], rec[:, qb % 2, :], lam_pair[:, :], ALU.mult))
                then(dve.tensor_scalar(probs[:, qb % 2, 1, 0:n], probs[:, qb % 2, 1, 0:n],
                                       rec[:, qb % 2, 1:2], None, ALU.mult))
                dve.scalar_tensor_tensor(probs[:, qb % 2, 0, 0:n], probs[:, qb % 2, 0, 0:n],
                                         rec[:, qb % 2, 0:1], probs[:, qb % 2, 1, 0:n],
                                         ALU.mult, ALU.add).then_inc(w_ready, 1)

            def split_weights(hd, qb):
                dve.wait_ge(wt_hi, 4 * hd + qb + 1)
                dve.tensor_tensor(h[:, WT0:WT0 + qb + 1, 1, qb * P:(qb + 1) * P],
                                  ps[:, STAT_BANK, 0:(qb + 1) * P].rearrange("p (k n) -> p k n", n=P),
                                  h[:, WT0:WT0 + qb + 1, 0, qb * P:(qb + 1) * P],
                                  ALU.subtract).then_inc(wt_ready, 1)

            def pool_windows(g):
                w = WINDOWS[g]
                u = probs[:, 0, 1, :]
                then(dve.tensor_copy(u, zbuf[:, PAD:]))
                src, dst = zbuf, gbuf
                for j in range(g + 1):
                    shift = 2 ** j
                    then(dve.tensor_tensor(dst[:, PAD:], src[:, PAD:], src[:, PAD - shift:PAD + T - shift],
                                           ALU.add))
                    src, dst = dst, src
                mean = pooled(g)
                then(dve.tensor_tensor(mean[:, 0:w], mean[:, 0:w], counts[:, 0:w], ALU.mult))
                dve.tensor_tensor(mean[:, 0:w], mean[:, 0:w], u[:, 0:w], ALU.subtract)
                dve.scalar_tensor_tensor(mean[:, w:], mean[:, w:], 1.0 / w, u[:, w:], ALU.mult,
                                         ALU.subtract).then_inc(pooled_new, 1)
                dve.wait_ge(pooled_hi, g + 1)
                dve.tensor_tensor(h[:, POOLED, 1, :], mean, h[:, POOLED, 0, :],
                                  ALU.subtract).then_inc(pooled_ready, 1)

            def even_mixer():
                r0 = start["even"]

                def split_ahead(n):
                    split_unit(r0 + 1 + (n + 2) // RING, (n + 2) % RING)

                split_unit(r0, 2)
                split_unit(r0, 3)
                split_unit(r0 + 1, 0)
                split_unit(r0 + 1, 1)
                norm_factors(1)
                then(dve.tensor_tensor(Rc2[:, :], Rc[:, :], Rc[:, :], ALU.mult))
                norm_rows(1)
                for tb in range(TB):
                    dve.wait_ge(v_hi, tb + 1)
                    dve.scalar_tensor_tensor(h[:, V0 + tb, 1, :], ps[:, V_BANK + tb, :], Rc[:, tb:tb + 1],
                                             h[:, V0 + tb, 0, :], ALU.mult, ALU.subtract).then_inc(v_ready, 1)
                for st in range(HEADS + 2):
                    cur, prev, older = st, st - 1, st - 2
                    if cur < HEADS:
                        split_ahead(3 * cur)
                        dve.wait_ge(q_hi, cur + 1)
                        dve.scalar_tensor_tensor(h[:, Q0 + cur % 2, 1, :], ps[:, Q_BANK, :],
                                                 cols[:, COL_QGAIN:COL_QGAIN + 1], h[:, Q0 + cur % 2, 0, :],
                                                 ALU.mult, ALU.subtract).then_inc(q_taken, 1)
                    if cur == 0:
                        dve.wait_ge(wpool_hi, 1)
                        dve.tensor_tensor(h[:, WPOOL, 1, :], acc[:, :], h[:, WPOOL, 0, :],
                                          ALU.subtract).then_inc(wpool_ready, 1)
                    if 0 <= older < HEADS:
                        dve.wait_ge(o_stats, older + 1)
                        dve.tensor_scalar(ms[:, :, 0:1], ps[:, STAT_BANK, 0:TB].unsqueeze(2), 1.0 / P, EPS,
                                          ALU.mult, ALU.add).then_inc(o_ms, 1)
                        inverse_root(1, o_ms, o_root, older + 1)
                        diagonal(obuf[:, :], rs[:, :, 0:1]).then_inc(o_diag, 1)
                    if 0 <= prev < HEADS:
                        dve.wait_ge(pool_hi, prev + 1)
                        dve.scalar_tensor_tensor(h[:, Y0 + HEADS + prev, 1, :], ps[:, POOL_BANK, :],
                                                 cols[:, COL_PSCALE + prev:COL_PSCALE + prev + 1],
                                                 h[:, Y0 + HEADS + prev, 0, :],
                                                 ALU.mult, ALU.subtract).then_inc(pool_ready, 1)
                        dve.wait_ge(qk_spread, prev + 1)
                        dve.tensor_tensor(ubuf[:, :], ubuf[:, :], ps[:, SPREAD_BANK, :],
                                          ALU.mult).then_inc(k_scaled, 1)
                        dve.wait_ge(k_hi, prev + 1)
                        dve.tensor_tensor(h[:, K0, 1, :], ubuf[:, :], h[:, K0, 0, :],
                                          ALU.subtract).then_inc(k_ready, 1)
                        row_maxima(prev, 0)
                        row_maxima(prev, 1)
                    if cur < HEADS:
                        split_ahead(3 * cur + 1)
                        dve.wait_ge(w_used, units_used(r0 + 1, 3 * cur + 1))
                        if cur:
                            dve.wait_ge(k_ready, cur)
                        dve.tensor_scalar(ubuf[:, :], ps[:, K_BANK, :], cols[:, COL_KGAIN:COL_KGAIN + 1],
                                          None, ALU.mult).then_inc(k_taken, 1)
                    if 0 <= prev < HEADS:
                        combine(prev, 0)
                        split_weights(prev, 0)
                        row_maxima(prev, 2)
                        combine(prev, 1)
                        split_weights(prev, 1)
                        row_maxima(prev, 3)
                    if 0 <= older < HEADS:
                        dve.wait_ge(o_spread, older + 1)
                        dve.tensor_tensor(acc[:, :], acc[:, :], ps[:, SPREAD_BANK, :],
                                          ALU.mult).then_inc(o_scaled, 1)
                        dve.wait_ge(y_hi, older + 1)
                        dve.tensor_tensor(h[:, Y0 + older, 1, :], acc[:, :], h[:, Y0 + older, 0, :],
                                          ALU.subtract).then_inc(y_ready, 1)
                    if 0 <= prev < HEADS:
                        combine(prev, 2)
                    if cur < HEADS:
                        split_ahead(3 * cur + 2)
                        dve.wait_ge(w_used, units_used(r0 + 1, 3 * cur + 2))
                        dve.tensor_tensor(zbuf[:, PAD:], ps[:, U_BANK, :], R[:, :], ALU.mult).then_inc(u_taken, 1)
                    if 0 <= prev < HEADS:
                        split_weights(prev, 2)
                        combine(prev, 3)
                        split_weights(prev, 3)
                        dve.wait_ge(o_sq, prev + 1)
                        dve.tensor_scalar(acc[:, :], ps[:, SPREAD_BANK, :], sub_gain[:, 0:1], None,
                                          ALU.mult).then_inc(o_taken, 1)
                    if cur < HEADS:
                        dve.wait_ge(qk_stats, cur + 1)
                        then(dve.tensor_tensor(ms[:, :, :], ps[:, STAT_BANK, 0:16].rearrange("p (b c) -> p b c", b=TB),
                                               Rc2[:, :].unsqueeze(2).to_broadcast([P, TB, 4]), ALU.mult))
                        dve.tensor_scalar(ms[:, :, :], ms[:, :, :], 1.0 / HD, EPS, ALU.mult,
                                          ALU.add).then_inc(qk_ms, 1)
                        inverse_root(4, qk_ms, qk_root, cur + 1)
                        then(dve.tensor_tensor(rs[:, :, :], rs[:, :, :],
                                               Rc[:, :].unsqueeze(2).to_broadcast([P, TB, 4]), ALU.mult))
                        for c in range(2):
                            last = diagonal(sq_qk[:, c, :], rs[:, :, 2 + c:3 + c])
                        last.then_inc(qk_diag, 1)
                        dve.tensor_scalar(qscale[:, :, :], rs[:, :, 0:2], HD ** -0.5, None, ALU.mult)
                        then(dve.tensor_scalar(nqscale[:, :, :], rs[:, :, 0:2], -HD ** -0.5, None, ALU.mult))
                        dve.wait_ge(u_taken, cur + 1)
                        pool_windows(cur)
                dve.wait_ge(y_ready, HEADS)
                clear_acc()
                out_projection("even_out", 2)

            def odd_mixer():
                r0 = start["odd"]

                def group(g, s, next_blocks=6, stats=False, more=True):
                    banks = GROUP_BANKS[s]
                    if stats:
                        split_unit(r0, 2, 6)
                        split_unit(r0, 3, 6)
                        norm_factors(4)
                    split_unit(r0 + g + 1, 0, next_blocks)
                    split_unit(r0 + g + 1, 1, next_blocks)
                    if stats:
                        norm_rows(4)
                    dve.wait_ge(w_used, units_used(r0 + g, RING - 1))
                    dve.tensor_tensor(gbuf[:, PAD:], ps[:, banks[1], :], R[:, :], ALU.mult)
                    dve.tensor_tensor(ubuf[:, :], ps[:, banks[2], :], R[:, :], ALU.mult).then_inc(conv_step, 1)
                    dve.tensor_tensor(obuf[:, :], ps[:, banks[0], :], R[:, :], ALU.mult).then_inc(group_taken, 1)
                    dve.wait_ge(conv_step, 5 * g + 1)
                    dve.tensor_tensor(zbuf[:, PAD:], gbuf[:, PAD:], ubuf[:, :], ALU.mult).then_inc(conv_step, 1)
                    dve.wait_ge(conv_step, 5 * g + 2)
                    if more:
                        split_unit(r0 + g + 1, 2, 6)
                    for j in range(CONV):
                        shifted = zbuf[:, PAD - (CONV - 1 - j):PAD - (CONV - 1 - j) + T]
                        tap = cols[:, bass.ds(g + (COL_CONV + NB * j), 1)]
                        if j == 0:
                            dve.tensor_scalar(sqbuf[:, :], shifted, tap, None, ALU.mult).then_inc(conv_step, 1)
                        else:
                            dve.scalar_tensor_tensor(sqbuf[:, :], shifted, tap, sqbuf[:, :], ALU.mult,
                                                     ALU.add).then_inc(conv_step, 1)
                        dve.wait_ge(conv_step, 5 * g + 3 + j)
                    dve.tensor_tensor(obuf[:, :], obuf[:, :], sqbuf[:, :], ALU.mult).then_inc(conv_new, 1)
                    dve.wait_ge(conv_hi, g + 1)
                    dve.tensor_tensor(h[:, Y0 + g, 1, :], obuf[:, :], h[:, Y0 + g, 0, :],
                                      ALU.subtract).then_inc(conv_ready, 1)
                    if more:
                        split_unit(r0 + g + 1, 3, 6)

                group(0, 0, stats=True)
                group(1, 1)
                with dve.Fori(1, NB // 2 - 1) as i:
                    group(2 * i, 0)
                    group(2 * i + 1, 1)
                group(NB - 2, 0)
                group(NB - 1, 1, next_blocks=NB, more=False)
                clear_acc()
                out_projection("odd_out", 5)

            dve.wait_ge(cols_ps, 1)
            dve.tensor_copy(cols[:, 0:NB], ps[:, SPREAD_BANK, 0:NB]).then_inc(cols_ready, 1)
            for m in range(NB):
                dve.wait_ge(xT_ps, m + 1)
                dve.tensor_copy(x[:, m, :], ps[:, m, :]).then_inc(x_new, 1)
                if m:
                    rest_of_gx(0, m - 1)
                for slot in FIRST_SPLITS[m]:
                    split_unit(0, slot)
            rest_of_gx(0, NB - 1)
            dve.wait_ge(cols_ps, 2)
            dve.tensor_copy(cols[:, NB:N_COLS], ps[:, SPREAD_BANK, NB:N_COLS]).then_inc(cols_ready, 1)
            dve.wait_ge(cols_ready, 2)
            dve.tensor_scalar(sub_gain[:, :], cols[:, COL_SUB:COL_SUB + 1], 1.0 - LAM_INIT, None, ALU.mult)
            ffn(0)
            even_mixer()
            ffn(1)
            ffn(2)
            odd_mixer()
            ffn(3)


_INS = ["x", "ffn1_norm", "ffn1_w_gate", "ffn1_w_up", "ffn1_w_down", "ffn2_norm", "ffn2_w_gate", "ffn2_w_up",
        "ffn2_w_down", "mix_norm", "even_w_in", "even_w_out", "q_gain", "k_gain", "subln_gain", "lambda_q1",
        "lambda_k1", "lambda_q2", "lambda_k2", "w_pool", "pool_scale", "odd_w_in", "conv_w", "odd_w_out"]
_OUT = ((1, T, D), "float32")


def kernel(**inputs):
    import numpy as _np
    import concourse.bacc as _bacc
    from concourse import mybir as _mybir
    from concourse.bass_utils import run_bass_kernel_spmd as _run

    nc = _bacc.Bacc("TRN2", target_bir_lowering=False, num_devices=1,
                    dynamic_dma_scratch_size=2048)
    arrays, args = {}, []
    for name in _INS:
        a = _np.ascontiguousarray(inputs[name])
        arrays[f"in_{name}"] = a
        args.append(nc.dram_tensor(f"in_{name}", a.shape, _mybir.dt.from_np(a.dtype), kind="ExternalInput").ap())
    shape, dtype = _OUT
    out = nc.dram_tensor("out", shape, _mybir.dt.from_np(_np.dtype(dtype)), kind="ExternalOutput").ap()
    build(nc, *args, out)
    r = _run(nc, [arrays], core_ids=[0])
    return r.results[0]["out"]
```

```python
from contextlib import ExitStack

import concourse.bass as bass
from concourse import mybir

F32 = mybir.dt.float32
F32R = mybir.dt.float32r
ALU = mybir.AluOpType
ACT = mybir.ActivationFunctionType
AX_X = mybir.AxisListType.X

P = 128
D = 1024
T = 512
FF = 2816
NB = D // P
TB = T // P
FT = FF // P
HEADS = 4
HD = 64
WINDOWS = (2, 4, 8, 16)
CONV = 3
EPS = 1e-6
LAM_INIT = 0.8 - 0.6
MASKED = -1e30
RING = 4
UNIT = 8 * P
PAD = 8

DOWN_UNITS = (6, 6, 5, 5)
DOWN_FIRST = (0, 6, 12, 17)


GATE_BANKS = (0, 2)
RES_BANKS = (4, 5)
GROUP_BANKS = ((0, 1, 2), (3, 6, 7))
STAT_BANK = 6
SPREAD_BANK = 7
Q_BANK = U_BANK = 0
K_BANK = 1
V_BANK = 2
SCORE_BANKS = (2, 4)
WT_BANKS = (6, 6, 7, 6)
HEAD_STAT_BANK = 2
K_SPREAD_BANK = 3
O_SPREAD_BANK = 4
POOL_BANK = 5
O_BANK = 7
O_STAT_BANK = 6
EVEN_TILE_BANKS = (0, 1, 3, 2, 4, 5, 4, 5)
OUT_BANKS = (6, 7)

WT0, Y0, V0, Q0, K0, POOLED, WPOOL = 1, 5, 13, 17, 19, 20, 21
NORM_ROWS = 6 * NB
COL_CONV = NORM_ROWS
COL_PSCALE = COL_CONV + CONV * NB
COL_QGAIN = COL_PSCALE + HEADS
COL_KGAIN, COL_SUB, N_COLS = COL_QGAIN + 1, COL_QGAIN + 2, COL_QGAIN + 3


def build(nc, x_in, ffn1_norm, ffn1_w_gate, ffn1_w_up, ffn1_w_down, ffn2_norm, ffn2_w_gate,
          ffn2_w_up, ffn2_w_down, mix_norm, even_w_in, even_w_out, q_gain, k_gain, subln_gain,
          lambda_q1, lambda_k1, lambda_q2, lambda_k2, w_pool, pool_scale, odd_w_in, conv_w,
          odd_w_out, out):
    start, rounds = {}, 0
    for name, units in (("ffn0", 2 * FT + 4 * NB), ("even", 4 + 3 * HEADS), ("even_out", NB),
                        ("ffn1", 2 * FT + 4 * NB), ("ffn2", 2 * FT + 4 * NB), ("odd", 4 * NB),
                        ("odd_out", NB), ("ffn3", 2 * FT + 4 * NB)):
        assert units % RING == 0
        start[name] = rounds
        rounds += units // RING
    FFNS = ((ffn1_w_gate, ffn1_w_up, ffn1_w_down, 0, 1), (ffn2_w_gate, ffn2_w_up, ffn2_w_down, 0, 3),
            (ffn1_w_gate, ffn1_w_up, ffn1_w_down, 1, 4), (ffn2_w_gate, ffn2_w_up, ffn2_w_down, 1, 6))

    with ExitStack() as ctx:
        def sb(name, shape, dt=F32):
            return ctx.enter_context(nc.sbuf_tensor(name, shape, dt))

        def sem(name):
            return ctx.enter_context(nc.semaphore(name))

        with nc.sbuf_tensor("x_tok", [P, TB, D], F32) as x_tok:
            pass
        with nc.sbuf_tensor("sq_qk", [P, 2, T], F32) as sq_qk:
            pass
        h = sb("h", [P, FT, 2, T], F32R)
        x = sb("x", [P, NB, T])
        gx = sb("gx", [P, NB, 2, T], F32R)
        raw = sb("raw", [P, RING, UNIT])
        whi = sb("whi", [P, RING, UNIT], F32R)
        wlo = sb("wlo", [P, RING, UNIT], F32R)
        R = sb("R", [P, T])
        acc = sb("acc", [P, T])
        gbuf = sb("gbuf", [P, PAD + T])
        zbuf = sb("zbuf", [P, PAD + T])
        ubuf = sb("ubuf", [P, T])
        tbuf = sb("tbuf", [P, PAD + T])
        sqbuf = sb("sqbuf", [P, T])
        obuf = sb("obuf", [P, T])
        probs = sb("probs", [P, 2, 2, T])
        ident = sb("ident", [P, P])
        ones = sb("ones", [P, P])
        mask = sb("mask", [P, P])
        halves = sb("halves", [P, 2])
        rows = sb("rows", [N_COLS, P])
        cols = sb("cols", [P, N_COLS])
        counts = sb("counts", [P, 16])
        ms = sb("ms", [P, TB, 5])
        sd = sb("sd", [P, TB, 5])
        rs = sb("rs", [P, TB, 5])
        nt = sb("nt", [P, TB, 5])
        Rc = sb("Rc", [P, TB])
        Rc2 = sb("Rc2", [P, TB])
        qscale = sb("qscale", [P, TB, 2])
        nqscale = sb("nqscale", [P, TB, 2])
        mx = sb("mx", [P, 2, 2])
        nbias = sb("nbias", [P, 2, 2])
        sums = sb("sums", [P, 2, 2])
        rec = sb("rec", [P, 2, 2])
        lam_rows = sb("lam_rows", [P, 4, HD])
        lam_prod = sb("lam_prod", [P, 2, HD])
        lam_sum = sb("lam_sum", [P, 2])
        lam_exp = sb("lam_exp", [P, 2])
        lam_pair = sb("lam_pair", [P, 2])
        sub_gain = sb("sub_gain", [P, 1])
        ps = ctx.enter_context(nc.psum_tensor("ps", [P, 8, T], F32))

        raw_in = [sem(f"raw_in{i}") for i in range(RING)]
        x_loaded = [sem(f"x_loaded{i}") for i in range(TB)]
        stored = [sem(f"stored{i}") for i in range(2)]
        (first_gains_in, params_in, lam_in, wpool_in, consts, cols_ps, cols_ready, lam_sum_ready, lam_exp_ready,
         hi_done, lo_done, w_used, xT_ps, x_new, xhi_done, sq_done, sq_added, gx_ready,
         norm_stats, norm_ms, norm_root, norm_diag, norm_spread, norm_ready,
         gate_scaled, up_scaled, silu_done, h_new, hhi_done, h_ready,
         v_hi, v_ready, q_hi, q_sq, q_taken, k_sq, k_taken, u_taken,
         head_stats, head_ms, head_root, qk_diag, qk_spread, k_scaled, k_hi, k_ready,
         scores_ready, bias_ready, exp_done, w_ready, wt_ps, wt_hi, wt_ready,
         o_ps, o_sq, o_taken, o_diag, o_spread, o_scaled, y_hi, y_ready,
         wpool_hi, wpool_ready, pooled_new, pooled_hi, pooled_ready, pool_ps, pool_hi, pool_ready,
         group_taken, acc_zero, window_step, conv_step, conv_new, conv_hi, conv_ready, fin_ready, outT_ps, outT_copied, step) = [
            sem(name) for name in (
                "first_gains_in params_in lam_in wpool_in consts cols_ps cols_ready lam_sum_ready lam_exp_ready "
                "hi_done lo_done w_used xT_ps x_new xhi_done sq_done sq_added gx_ready "
                "norm_stats norm_ms norm_root norm_diag norm_spread norm_ready "
                "gate_scaled up_scaled silu_done h_new hhi_done h_ready "
                "v_hi v_ready q_hi q_sq q_taken k_sq k_taken u_taken "
                "head_stats head_ms head_root qk_diag qk_spread k_scaled k_hi k_ready "
                "scores_ready bias_ready exp_done w_ready wt_ps wt_hi wt_ready "
                "o_ps o_sq o_taken o_diag o_spread o_scaled y_hi y_ready "
                "wpool_hi wpool_ready pooled_new pooled_hi pooled_ready pool_ps pool_hi pool_ready "
                "group_taken acc_zero window_step conv_step conv_new conv_hi conv_ready fin_ready outT_ps outT_copied step").split()]
        FIRST_SPLITS = (("x", 0), ("x", 1), ("unit", 0), ("x", 2), ("x", 3), ("unit", 1), ("x", 4), ("unit", 2),
                        ("x", 5), ("unit", 3), ("x", 6), ("x", 7))
        N_CONSTS = 12
        N_PARAMS = 10

        def loaded(rnd, phase):
            if phase == "odd":
                return 32 * (rnd + 1) + -16 * start["odd"]
            return 16 * (rnd + 1) + (16 * NB if phase in ("odd_out", "ffn3") else 0)

        def units_used(rnd, slot):
            return RING * rnd + slot + 1

        def spread_cols(src):
            return src.unsqueeze(2).to_broadcast([P, TB, P])

        def first_squares(m):
            return (sqbuf, obuf)[m % 2]

        def fin(s):
            return (sqbuf, obuf)[s]

        def pooled(g):
            return (gbuf, zbuf)[g % 2][:, PAD:]

        block = ctx.enter_context(nc.Block())

        @block.sync
        def _(sp):
            def load(rnd, slot, *parts, first=False):
                if not first:
                    sp.wait_ge(lo_done, RING * (rnd - 1) + slot + 1)
                at = 0
                for src in parts:
                    _, blocks, n = src.shape
                    sp.dma_start(raw[:, slot, at:at + blocks * n].rearrange("p (a n) -> p a n", a=blocks),
                                 src).then_inc(raw_in[slot], 16)
                    at += blocks * n

            def columns(w, col, first_block=0, blocks=NB, width=P):
                return w.rearrange("(c p) n -> p c n", p=P)[:, first_block:first_block + blocks,
                                                            bass.ds(col, width)]

            def row_load(row, src, loads):
                sp.dma_start(rows[row:row + src.shape[0], :], src).then_inc(loads, 16)

            def parameters():
                for r, src in ((1, mix_norm[0]), (2, ffn2_norm[0]), (3, ffn1_norm[1]), (4, mix_norm[1]),
                               (5, ffn2_norm[1])):
                    row_load(NB * r, src.rearrange("(c p) -> c p", p=P), params_in)
                row_load(COL_CONV, conv_w[0].rearrange("j (c p) -> (j c) p", p=P), params_in)
                row_load(COL_PSCALE, pool_scale[0].rearrange("(c p) -> c p", p=P), params_in)
                for row, src in ((COL_QGAIN, q_gain), (COL_KGAIN, k_gain)):
                    sp.dma_start(rows[row:row + 1, :].rearrange("a (c p) -> a c p", c=2),
                                 src.unsqueeze(1).to_broadcast([1, 2, HD])).then_inc(params_in, 16)
                row_load(COL_SUB, subln_gain, params_in)
                for j, src in enumerate((lambda_q1, lambda_q2, lambda_k1, lambda_k2)):
                    sp.dma_start(lam_rows[:, j, :], src.to_broadcast([P, HD])).then_inc(lam_in, 16)

            def ffn(f):
                w_gate, w_up, w_down, layer, _ = FFNS[f]
                r0 = start[f"ffn{f}"]
                r1 = r0 + FT // 2

                def two_tiles(i, first=False):
                    for s in range(2):
                        load(r0 + i, 2 * s, columns(w_gate[layer], (2 * i + s) * P), first=first)
                        load(r0 + i, 2 * s + 1, columns(w_up[layer], (2 * i + s) * P), first=first)

                if f == 0:
                    two_tiles(0, first=True)
                    parameters()
                with sp.Fori(1 if f == 0 else 0, FT // 2) as i:
                    two_tiles(i)
                with sp.Fori(0, NB) as m:
                    for s in range(RING):
                        load(r1 + m, s, columns(w_down[layer], m * P, DOWN_FIRST[s], DOWN_UNITS[s]))

            def out_projection(name, w):
                with sp.Fori(0, NB // RING) as i:
                    for s in range(RING):
                        load(start[name] + i, s, columns(w, (RING * i + s) * P))

            row_load(0, ffn1_norm[0].rearrange("(c p) -> c p", p=P), first_gains_in)
            for tb in range(TB):
                sp.dma_start(x_tok[:, tb, :], x_in[0, tb * P:(tb + 1) * P, :]).then_inc(x_loaded[tb], 16)
            ffn(0)
            r0 = start["even"]
            for s in range(RING):
                load(r0, s, columns(even_w_in[0], 2 * T, 2 * s, 2, T))
            for n in range(3 * HEADS):
                head, kind = divmod(n, 3)
                load(r0 + 1 + n // RING, n % RING, columns(even_w_in[0], (0, T, 3 * T)[kind] + head * P))
                if n == 2:
                    sp.wait_ge(norm_ms, 2)
                    sp.dma_start(acc[:, :].rearrange("p (g d) -> p g d", g=HEADS),
                                 w_pool[0].rearrange("g c d -> c g d")).then_inc(wpool_in, 16)
            out_projection("even_out", even_w_out[0])
            ffn(1)
            ffn(2)
            w_bch = odd_w_in[0].rearrange("(c p) (k n) -> p c k n", p=P, k=3)
            with sp.Fori(0, NB) as g:
                for s in range(RING):
                    load(start["odd"] + g, s, *(w_bch[:, 2 * s + j, :, bass.ds(g * P, P)] for j in range(2)))
            out_projection("odd_out", odd_w_out[0])
            ffn(3)
            for s in range(2):
                sp.wait_ge(stored[s], 16 * (NB // 2))

        @block.gpsimd
        def _(pool):
            pool.memset(ones[:, :], 1.0).then_inc(consts, 1)
            pool.memset(ident[:, :], 0.0).then_inc(consts, 1)
            pool.memset(mask[:, :], 0.0).then_inc(consts, 1)
            pool.memset(halves[:, :], 0.0).then_inc(consts, 1)
            pool.memset(gbuf[:, 0:PAD], 0.0).then_inc(consts, 1)
            pool.memset(zbuf[:, 0:PAD], 0.0).then_inc(consts, 1)
            pool.memset(tbuf[:, 0:PAD], 0.0).then_inc(consts, 1)
            pool.wait_ge(consts, 7)
            pool.affine_select(out=ident[:, :], in_=ident[:, :], compare_op=ALU.not_equal, fill=1.0,
                               base=0, pattern=[[-1, P]], channel_multiplier=1).then_inc(consts, 1)
            pool.affine_select(out=mask[:, :], in_=mask[:, :], compare_op=ALU.is_ge, fill=MASKED,
                               base=0, pattern=[[-1, P]], channel_multiplier=1).then_inc(consts, 1)
            pool.wait_ge(consts, 9)
            pool.memset(halves[0:HD, 0:1], 1.0).then_inc(consts, 1)
            pool.wait_ge(consts, 10)
            pool.memset(halves[HD:P, 1:2], 1.0).then_inc(consts, 1)
            pool.wait_ge(consts, 11)
            for t in range(max(WINDOWS)):
                last = pool.memset(counts[:, t:t + 1], 1.0 / (t + 1))
            last.then_inc(consts, 1)
            pool.memset(acc[:, :], 0.0).then_inc(acc_zero, 1)
            pool.wait_ge(acc_zero, 1)
            for m in range(NB):
                pool.wait_ge(sq_done, m + 1)
                pool.tensor_tensor(acc[:, :], acc[:, :], first_squares(m)[:, :], ALU.add).then_inc(sq_added, 1)
                pool.wait_ge(sq_added, m + 1)

            steps = [0]

            def then(instruction):
                steps[0] += 1
                instruction.then_inc(window_step, 1)
                pool.wait_ge(window_step, steps[0])

            def pool_windows(g):
                w = WINDOWS[g]
                pool.wait_ge(u_taken, g + 1)
                if g:
                    pool.wait_ge(pooled_ready, g)
                src = tbuf
                for j in range(g + 1):
                    shift, dst = 2 ** j, (gbuf, zbuf)[j % 2]
                    then(pool.tensor_tensor(dst[:, PAD:], src[:, PAD:], src[:, PAD - shift:PAD + T - shift],
                                            ALU.add))
                    src = dst
                mean = pooled(g)
                then(pool.tensor_tensor(mean[:, 0:w], mean[:, 0:w], counts[:, 0:w], ALU.mult))
                then(pool.tensor_scalar(mean[:, w:], mean[:, w:], 1.0 / w, None, ALU.mult))
                pool.tensor_tensor(mean, mean, tbuf[:, PAD:], ALU.subtract).then_inc(pooled_new, 1)
                pool.wait_ge(pooled_hi, g + 1)
                pool.tensor_tensor(h[:, POOLED, 1, :], mean, h[:, POOLED, 0, :],
                                   ALU.subtract).then_inc(pooled_ready, 1)

            def split_units(first, end):
                for n in range(first, end):
                    slot = n % RING
                    pool.wait_ge(hi_done, RING * (start["even"] + 1) + n + 1)
                    pool.wait_ge(lo_done, RING * (start["even"] + 1) + n)
                    pool.tensor_tensor(wlo[:, slot, :], raw[:, slot, :], whi[:, slot, :],
                                       ALU.subtract).then_inc(lo_done, 1)

            for c in range(HEADS):
                if c:
                    pool_windows(c - 1)
                split_units(3 * c + 2, 3 * c + 5)
            split_units(3 * HEADS + 2, 3 * HEADS + 4)
            pool_windows(HEADS - 1)

        @block.tensor
        def _(pe):
            def product(dst, lhs, rhs, begin, end):
                pe.matmul(dst, lhs[0], rhs[0], start=begin, stop=False)
                pe.matmul(dst, lhs[0], rhs[1], start=False, stop=False)
                return pe.matmul(dst, lhs[1], rhs[0], start=False, stop=end)

            def weight(slot, i, n=P):
                return whi[:, slot, i * n:(i + 1) * n], wlo[:, slot, i * n:(i + 1) * n]

            def gxb(k, a=0, b=T):
                return gx[:, k, 0, a:b], gx[:, k, 1, a:b]

            def hb(k, a=0, b=T, p0=0, p1=P):
                return h[p0:p1, k, 0, a:b], h[p0:p1, k, 1, a:b]

            def column_block(rnd, slot, bank, norm=None):
                pe.wait_ge(lo_done, RING * rnd + slot + 1)
                for k in range(NB):
                    if norm is not None:
                        pe.wait_ge(gx_ready, NB * norm + k + 1)
                    last = product(ps[:, bank, :], weight(slot, k), gxb(k), k == 0, k == NB - 1)
                last.then_inc(w_used, 1)

            def stats_of_norm(r):
                pe.wait_ge(sq_added, NB * (r + 1))
                for tb in range(TB):
                    last = pe.matmul(ps[:, STAT_BANK, tb:tb + 1], acc[:, tb * P:(tb + 1) * P], ones[:, 0:1],
                                     start=True, stop=True)
                last.then_inc(norm_stats, 1)

            def spread_of_norm(r):
                pe.wait_ge(norm_diag, r + 1)
                pe.matmul(ps[:, SPREAD_BANK, :], ones[:, :], obuf[:, :], start=True,
                          stop=True).then_inc(norm_spread, 1)

            def transpose_result(m, s, first=False):
                pe.wait_ge(fin_ready, m + 1)
                if not first:
                    pe.wait_ge(outT_copied, m - 1)
                for tb in range(TB):
                    last = pe.transpose(ps[:, OUT_BANKS[s], tb * P:(tb + 1) * P],
                                        fin(s)[:, tb * P:(tb + 1) * P], ident[:, :])
                last.then_inc(outT_ps, 1)

            def ffn(f):
                phase = FFNS[f][4]
                r0 = start[f"ffn{f}"]
                r1 = r0 + FT // 2

                def two_tiles(i, first=False):
                    for s in range(2):
                        new = first and s == 0
                        if not first:
                            pe.wait_ge(up_scaled, FT * f + 2 * i + s - 1)
                        column_block(r0 + i, 2 * s, GATE_BANKS[s], phase - 1 if new else None)
                        if new:
                            stats_of_norm(phase - 1)
                        column_block(r0 + i, 2 * s + 1, GATE_BANKS[s] + 1)
                        if new:
                            spread_of_norm(phase - 1)

                def first_tiles():
                    for part in range(2):
                        for n in range(RING):
                            if part == 0:
                                pe.wait_ge(lo_done, n + 1)
                            for k in range(part * NB // 2, (part + 1) * NB // 2):
                                if n == 0:
                                    pe.wait_ge(gx_ready, k + 1)
                                last = product(ps[:, n, :], weight(n, k), gxb(k), k == 0, k == NB - 1)
                            if part == 1:
                                last.then_inc(w_used, 1)
                            if part == 1 and n == 0:
                                pe.wait_ge(consts, N_CONSTS)
                                pe.wait_ge(params_in, 16 * N_PARAMS)
                                pe.transpose(ps[:, SPREAD_BANK, 0:N_COLS], rows[:, :],
                                             ident[0:N_COLS, 0:N_COLS]).then_inc(cols_ps, 1)
                                stats_of_norm(0)
                            if part == 1 and n == 1:
                                pe.wait_ge(cols_ready, 2)
                                spread_of_norm(0)

                def down_tile(m, s, first=False):
                    for q in range(RING):
                        pe.wait_ge(lo_done, RING * (r1 + m) + q + 1)
                        for j in range(DOWN_UNITS[q]):
                            k = DOWN_FIRST[q] + j
                            if first and k == FT - 1:
                                pe.wait_ge(h_ready, FT * (f + 1))
                            last = product(ps[:, RES_BANKS[s], :], weight(q, j), hb(k), k == 0, k == FT - 1)
                        last.then_inc(w_used, 1)

                if f == 0:
                    first_tiles()
                else:
                    two_tiles(0, first=True)
                with pe.Fori(1, FT // 2) as i:
                    two_tiles(i)
                pe.wait_ge(h_ready, FT * (f + 1) - 1)
                if f < 3:
                    pe.wait_ge(x_new, NB * phase - 1)
                    down_tile(0, 0, first=True)
                    pe.wait_ge(x_new, NB * phase)
                    down_tile(1, 1)
                    with pe.Fori(1, NB // 2) as i:
                        for s in range(2):
                            m = 2 * i + s
                            pe.wait_ge(x_new, NB * phase + m - 1)
                            down_tile(m, s)
                else:
                    down_tile(0, 0, first=True)
                    down_tile(1, 1)
                    for s in range(2):
                        transpose_result(s, s, first=True)
                        down_tile(2 + s, s)
                    with pe.Fori(2, NB // 2) as i:
                        for s in range(2):
                            m = 2 * i + s
                            transpose_result(m - 2, s)
                            down_tile(m, s)
                    transpose_result(NB - 2, 0)
                    transpose_result(NB - 1, 1)

            def output_part(name, m, bank, blocks, end=False):
                for k in blocks:
                    last = product(ps[:, bank, :], weight(m % RING, k), hb(Y0 + k), k == HEADS,
                                   end and k == blocks[-1])
                if end:
                    last.then_inc(w_used, 1)

            def output_split(name, m):
                pe.wait_ge(lo_done, RING * start[name] + m + 1)

            def scores(hd, qb):
                if qb >= 2:
                    pe.wait_ge(exp_done, 4 * hd + qb - 1)
                for c in range(2):
                    p0, p1 = c * HD, (c + 1) * HD
                    last = product(ps[:, SCORE_BANKS[qb % 2] + c, 0:(qb + 1) * P],
                                   hb(Q0 + hd % 2, qb * P, (qb + 1) * P, p0, p1),
                                   hb(K0, 0, (qb + 1) * P, p0, p1), True, True)
                last.then_inc(scores_ready, 1)

            def transpose_weights(hd, *qbs):
                for qb in qbs:
                    pe.wait_ge(w_ready, 4 * hd + qb + 1)
                    at = P if qb == 1 else 0
                    for kb in range(qb + 1):
                        last = pe.transpose(ps[:, WT_BANKS[qb], at + kb * P:at + (kb + 1) * P],
                                            probs[:, qb % 2, 0, kb * P:(kb + 1) * P], ident[:, :])
                last.then_inc(wt_ps, len(qbs))

            def statistics(bank, c=None, o=None):
                if o is not None:
                    pe.wait_ge(o_sq, o + 1)
                    for tb in range(TB):
                        last = pe.matmul(ps[:, bank, 16 + tb:17 + tb], sqbuf[:, tb * P:(tb + 1) * P],
                                         ones[:, 0:1], start=True, stop=True)
                if c is not None:
                    pe.wait_ge(q_sq, c + 1)
                    pe.wait_ge(k_sq, c + 1)
                    for j in range(2):
                        for tb in range(TB):
                            last = pe.matmul(ps[:, bank, 4 * tb + 2 * j:4 * tb + 2 * j + 2],
                                             sq_qk[:, j, tb * P:(tb + 1) * P], halves[:, :],
                                             start=True, stop=True)
                last.then_inc(head_stats, 1)

            def spread_k(c):
                pe.wait_ge(qk_diag, c + 1)
                for j in range(2):
                    last = pe.matmul(ps[j * HD:(j + 1) * HD, K_SPREAD_BANK, :], ones[:, 0:HD],
                                     sq_qk[:, j, :], start=True, stop=True)
                last.then_inc(qk_spread, 1)

            def spread_o(o):
                pe.wait_ge(o_diag, o + 1)
                pe.matmul(ps[:, O_SPREAD_BANK, :], ones[:, :], obuf[:, :], start=True,
                          stop=True).then_inc(o_spread, 1)

            def pool_product(g):
                pe.wait_ge(wpool_ready, 1)
                pe.wait_ge(pooled_ready, g + 1)
                product(ps[:, POOL_BANK, :], hb(WPOOL, g * P, (g + 1) * P), hb(POOLED), True,
                        True).then_inc(pool_ps, 1)

            def weigh_values(hd):
                pe.wait_ge(wt_ready, 4 * (hd + 1))
                for kb in range(TB):
                    last = product(ps[:, O_BANK, kb * P:T], hb(V0 + kb, hd * P, (hd + 1) * P),
                                   hb(WT0 + kb, kb * P, T), kb == 0, kb == TB - 1)
                last.then_inc(o_ps, 1)

            def even_mixer():
                r0 = start["even"]
                for s in range(RING):
                    pe.wait_ge(lo_done, RING * r0 + s + 1)
                    for j in range(2):
                        k = 2 * s + j
                        pe.wait_ge(gx_ready, NB + k + 1)
                        for tb in range(TB):
                            if k == 0 and V_BANK + tb in RES_BANKS:
                                pe.wait_ge(x_new, 2 * NB + V_BANK + tb - RES_BANKS[1])
                            last = product(ps[:, V_BANK + tb, :], gxb(k, tb * P, (tb + 1) * P),
                                           weight(s, j, T), k == 0, k == NB - 1)
                    last.then_inc(w_used, 1)
                stats_of_norm(1)

                def unit_of(n):
                    return r0 + 1 + n // RING, n % RING

                for c in range(HEADS + 1):
                    p, o = c - 1, c - 2
                    last_stage = c == HEADS
                    if p >= 0:
                        pe.wait_ge(k_ready, p + 1)
                        scores(p, 0)
                        if o >= 1:
                            pe.wait_ge(o_scaled, o)
                            pe.wait_ge(pool_ready, o + 1)
                        elif o == 0:
                            pe.wait_ge(pool_ready, 1)
                        scores(p, 1)
                    if not last_stage:
                        if c:
                            pe.wait_ge(u_taken, c)
                        column_block(*unit_of(3 * c), Q_BANK)
                    else:
                        pe.wait_ge(u_taken, HEADS)
                        output_split("even_out", 0)
                        pe.wait_ge(y_ready, HEADS - 2)
                        output_part("even_out", 0, EVEN_TILE_BANKS[0], (4, 5, 6, 0, 1))
                    if c == 0:
                        spread_of_norm(1)
                    if p >= 0:
                        if p:
                            pe.wait_ge(wt_ready, 4 * p)
                        transpose_weights(p, 0, 1)
                        scores(p, 2)
                        scores(p, 3)
                    if not last_stage:
                        column_block(*unit_of(3 * c + 1), K_BANK)
                    else:
                        output_split("even_out", 1)
                        output_part("even_out", 1, EVEN_TILE_BANKS[1], (4, 5, 6, 0, 1))
                    if p >= 0:
                        if p:
                            pe.wait_ge(o_taken, p)
                        transpose_weights(p, 2)
                        pe.wait_ge(wt_ready, 4 * p + 2)
                        transpose_weights(p, 3)
                    else:
                        pe.wait_ge(v_ready, TB)
                    statistics(HEAD_STAT_BANK, c=None if last_stage else c, o=o if o >= 0 else None)
                    if not last_stage:
                        pe.wait_ge(q_taken, c + 1)
                        column_block(*unit_of(3 * c + 2), U_BANK)
                        spread_k(c)
                    else:
                        output_split("even_out", 2)
                        output_part("even_out", 2, EVEN_TILE_BANKS[2], (4, 5, 6, 0, 1))
                    if o >= 0:
                        spread_o(o)
                    if p >= 0:
                        pool_product(p)
                        weigh_values(p)
                output_split("even_out", 3)
                pe.wait_ge(head_ms, HEADS + 1)
                output_part("even_out", 3, EVEN_TILE_BANKS[3], (4, 5, 6))
                statistics(O_STAT_BANK, o=HEADS - 1)
                pe.wait_ge(pool_ready, HEADS)
                pe.wait_ge(y_ready, HEADS - 1)
                for m in range(3):
                    output_part("even_out", m, EVEN_TILE_BANKS[m], (7, 2))
                spread_o(HEADS - 1)
                output_part("even_out", 3, EVEN_TILE_BANKS[3], (0, 1, 7, 2))
                pe.wait_ge(y_ready, HEADS)
                for m in range(NB):
                    if m >= RING:
                        output_split("even_out", m)
                    if m == 4 or m >= 6:
                        pe.wait_ge(x_new, 2 * NB + (1 if m == 4 else m - 1))
                    output_part("even_out", m, EVEN_TILE_BANKS[m], (3,) if m < RING else (4, 5, 6, 7, 0, 1, 2, 3),
                                end=True)

            def odd_mixer():
                r0 = start["odd"]

                def two_groups(i, first=False):
                    for s in range(2):
                        if not first:
                            pe.wait_ge(group_taken, 2 * i + s - 1)
                        if first and s == 1:
                            pe.wait_ge(norm_ready, 5)
                        for q in range(RING):
                            pe.wait_ge(lo_done, RING * (r0 + 2 * i + s) + q + 1)
                            for j in range(2):
                                k = 2 * q + j
                                if first and s == 0:
                                    pe.wait_ge(gx_ready, 4 * NB + k + 1)
                                for kind in range(3):
                                    last = product(ps[:, GROUP_BANKS[s][kind], :], weight(q, 3 * j + kind), gxb(k),
                                                   k == 0, k == NB - 1)
                            last.then_inc(w_used, 1)
                            if first and s == 0 and q == 1:
                                stats_of_norm(4)
                        if first and s == 0:
                            spread_of_norm(4)

                two_groups(0, True)
                with pe.Fori(1, NB // 2) as i:
                    two_groups(i)
                pe.wait_ge(conv_ready, NB - 1)
                early, every = (4, 5, 6, 0, 1, 2, 3), (4, 5, 6, 7, 0, 1, 2, 3)
                for m in range(2):
                    pe.wait_ge(x_new, 5 * NB + m - 1)
                    output_split("odd_out", m)
                    output_part("odd_out", m, RES_BANKS[m], early)
                pe.wait_ge(conv_ready, NB)
                for m in range(NB):
                    if m >= 2:
                        pe.wait_ge(x_new, 5 * NB + m - 1)
                        output_split("odd_out", m)
                    output_part("odd_out", m, RES_BANKS[m % 2], (7,) if m < 2 else every, end=True)

            pe.wait_ge(consts, 9)
            pe.wait_ge(first_gains_in, 16)
            pe.transpose(ps[:, SPREAD_BANK, 0:NB], rows[0:NB, :], ident[0:NB, 0:NB]).then_inc(cols_ps, 1)
            for tb in range(TB):
                pe.wait_ge(x_loaded[tb], 16)
                for m in range(NB):
                    if tb == 0 and m == SPREAD_BANK:
                        pe.wait_ge(cols_ready, 1)
                    tile = pe.transpose(ps[:, m, tb * P:(tb + 1) * P], x_tok[:, tb, m * P:(m + 1) * P],
                                        ident[:, :])
                    if tb == TB - 1:
                        tile.then_inc(xT_ps, 1)
            ffn(0)
            even_mixer()
            ffn(1)
            ffn(2)
            odd_mixer()
            ffn(3)

        @block.scalar
        def _(act):
            def round_unit(rnd, slot, blocks=NB, first=False, phase=None):
                act.wait_ge(raw_in[slot], loaded(rnd, phase))
                if not first:
                    act.wait_ge(w_used, units_used(rnd - 1, slot))
                act.activation(whi[:, slot, 0:blocks * P], raw[:, slot, 0:blocks * P],
                               ACT.Copy).then_inc(hi_done, 1)

            def residual(phase, m):
                g = NB * phase + m
                act.wait_ge(cols_ready, 2)
                act.wait_ge(x_new, g + 1)
                act.activation(gx[:, m, 0, :], x[:, m, :], ACT.Copy,
                               scale=cols[:, bass.ds(g, 1)]).then_inc(xhi_done, 1)
                act.wait_ge(cols_ready, 2)
                act.wait_ge(sq_added, g)
                act.activation(sqbuf[:, :], x[:, m, :], ACT.Square).then_inc(sq_done, 1)

            def root(ms_ready, count, a, b, done):
                act.wait_ge(ms_ready, count)
                act.activation(sd[:, :, a:b], ms[:, :, a:b], ACT.Sqrt).then_inc(done, 1)

            def ffn(f):
                phase = FFNS[f][4]
                r0 = start[f"ffn{f}"]
                r1 = r0 + FT // 2

                def activate(t):
                    act.wait_ge(gate_scaled, FT * f + t + 1)
                    act.activation(gbuf[:, PAD:], gbuf[:, PAD:], ACT.Silu).then_inc(silu_done, 1)
                    act.wait_ge(cols_ready, 1)
                    act.wait_ge(h_new, FT * f + t + 1)
                    act.activation(h[:, t, 0, :], ubuf[:, :], ACT.Copy).then_inc(hhi_done, 1)

                name = f"ffn{f}"

                def two_tiles(i, first=False):
                    if not first:
                        round_unit(r0 + i, 2, phase=name)
                        round_unit(r0 + i, 3, phase=name)
                    activate(2 * i)
                    round_unit(r0 + i + 1, 0, phase=name)
                    round_unit(r0 + i + 1, 1, phase=name)
                    activate(2 * i + 1)

                root(norm_ms, phase, 0, 1, norm_root)
                two_tiles(0, first=f == 0)
                if f == 0:
                    act.wait_ge(lam_sum_ready, 1)
                    act.activation(lam_exp[:, :], lam_sum[:, :], ACT.Exp).then_inc(lam_exp_ready, 1)
                with act.Fori(1, FT // 2 - 1) as i:
                    two_tiles(i)
                round_unit(r1 - 1, 2, phase=name)
                round_unit(r1 - 1, 3, phase=name)
                activate(FT - 2)
                for s in range(RING):
                    round_unit(r1, s, DOWN_UNITS[s], phase=name)
                activate(FT - 1)

                def next_tile(m):
                    for s in range(RING):
                        round_unit(r1 + m + 1, s, DOWN_UNITS[s], phase=name)

                if f < 3:
                    with act.Fori(0, NB - 1) as m:
                        next_tile(m)
                        residual(phase, m)
                else:
                    next_tile(0)
                    for s in range(2):
                        next_tile(s + 1)
                        store_result(s, s, first=True)
                    with act.Fori(1, NB // 2 - 1) as i:
                        for s in range(2):
                            next_tile(2 * i + s + 1)
                            store_result(2 * i + s, s)
                    store_result(NB - 2, 0)
                    store_result(NB - 1, 1)
                if f < 3:
                    blocks = 6 if f == 2 else NB
                    after = "odd" if f == 2 else None
                    round_unit(r1 + NB, 0, blocks, phase=after)
                    round_unit(r1 + NB, 1, blocks, phase=after)
                    residual(phase, NB - 1)

            def out_projection(name, phase, ahead):
                for m in range(NB):
                    if m + ahead < NB + 2:
                        round_unit(start[name] + (m + ahead) // RING, (m + ahead) % RING, phase=name)
                    residual(phase, m)

            def store_result(m, s, first=False):
                act.wait_ge(outT_ps, m + 1)
                if not first:
                    act.wait_ge(stored[s], 8 * m - 8 * s)
                act.activation(probs[:, s, 0, :], ps[:, OUT_BANKS[s], :], ACT.Copy).then_inc(outT_copied, 1)
                act.wait_ge(outT_copied, m + 1)
                act.dma_start(out[0].rearrange("(b p) d -> p b d", p=P)[:, :, bass.ds(m * P, P)],
                              probs[:, s, 0, :].rearrange("p (b n) -> p b n", b=TB)).then_inc(stored[s], 16)

            def exps(hd, qb):
                act.wait_ge(bias_ready, 4 * hd + qb + 1)
                if 4 * hd + qb >= 2:
                    act.wait_ge(wt_ps, 4 * hd + qb - 1)
                for c in range(2):
                    last = act.activation(probs[:, qb % 2, c, 0:(qb + 1) * P],
                                          ps[:, SCORE_BANKS[qb % 2] + c, 0:(qb + 1) * P], ACT.Exp,
                                          scale=qscale[:, qb, c:c + 1], bias=nbias[:, qb % 2, c:c + 1],
                                          accum_out=sums[:, qb % 2, c:c + 1])
                last.then_inc(exp_done, 1)

            def round_weights(hd, *qbs):
                act.wait_ge(wt_ps, 4 * hd + qbs[-1] + 1)
                if qbs[0] == 0 and hd:
                    act.wait_ge(o_ps, hd)
                for qb in qbs:
                    at = P if qb == 1 else 0
                    last = act.activation(h[:, WT0:WT0 + qb + 1, 0, qb * P:(qb + 1) * P],
                                          ps[:, WT_BANKS[qb], at:at + (qb + 1) * P].rearrange(
                                              "p (k n) -> p k n", n=P), ACT.Copy)
                last.then_inc(wt_hi, len(qbs))

            def even_mixer():
                r0 = start["even"]

                def round_unit_of(n):
                    round_unit(r0 + 1 + n // RING, n % RING)

                round_unit(r0, 2)
                round_unit(r0, 3)
                round_unit_of(0)
                round_unit_of(1)
                root(norm_ms, 2, 0, 1, norm_root)
                act.wait_ge(norm_diag, 2)
                for tb in range(TB):
                    act.activation(h[:, V0 + tb, 0, :], ps[:, V_BANK + tb, :], ACT.Copy,
                                   scale=Rc[:, tb:tb + 1]).then_inc(v_hi, 1)
                for c in range(HEADS + 1):
                    p, o = c - 1, c - 2
                    if p >= 0:
                        exps(p, 0)
                        exps(p, 1)
                    if c < HEADS:
                        round_unit_of(3 * c + 2)
                        act.wait_ge(w_used, units_used(r0 + 1, 3 * c))
                        act.activation(h[:, Q0 + c % 2, 0, :], ps[:, Q_BANK, :], ACT.Copy,
                                       scale=cols[:, COL_QGAIN:COL_QGAIN + 1]).then_inc(q_hi, 1)
                    else:
                        round_unit_of(3 * c + 2)
                        round_unit_of(3 * c + 3)
                    if c == 0:
                        act.wait_ge(wpool_in, 16)
                        act.activation(h[:, WPOOL, 0, :], acc[:, :], ACT.Copy).then_inc(wpool_hi, 1)
                    if p >= 0:
                        round_weights(p, 0, 1)
                    if c < HEADS:
                        if c:
                            act.wait_ge(qk_spread, c)
                        act.wait_ge(q_taken, c + 1)
                        act.activation(sq_qk[:, 0, :], ps[:, Q_BANK, :], ACT.Square).then_inc(q_sq, 1)
                        round_unit_of(3 * c + 3)
                    if p >= 0:
                        exps(p, 2)
                        act.wait_ge(pooled_new, p + 1)
                        act.activation(h[:, POOLED, 0, :], pooled(p), ACT.Copy).then_inc(pooled_hi, 1)
                        exps(p, 3)
                    if c < HEADS:
                        round_unit_of(3 * c + 4)
                        act.wait_ge(w_used, units_used(r0 + 1, 3 * c + 1))
                        if c:
                            act.wait_ge(k_ready, c)
                        act.activation(ubuf[:, :], ps[:, K_BANK, :], ACT.Copy,
                                       scale=cols[:, COL_KGAIN:COL_KGAIN + 1]).then_inc(k_taken, 1)
                        act.activation(sq_qk[:, 1, :], ps[:, K_BANK, :], ACT.Square).then_inc(k_sq, 1)
                    if p >= 0:
                        round_weights(p, 2)
                        round_weights(p, 3)
                    a, b = 0 if c < HEADS else 4, 5 if o >= 0 else 4
                    root(head_ms, c + 1, a, b, head_root)
                    if c < HEADS:
                        act.wait_ge(k_scaled, c + 1)
                        act.activation(h[:, K0, 0, :], ubuf[:, :], ACT.Copy).then_inc(k_hi, 1)
                    if o >= 0:
                        round_y(o)
                    if p >= 0:
                        act.wait_ge(pool_ps, p + 1)
                        act.activation(h[:, Y0 + HEADS + p, 0, :], ps[:, POOL_BANK, :], ACT.Copy,
                                       scale=cols[:, COL_PSCALE + p:COL_PSCALE + p + 1]).then_inc(pool_hi, 1)
                        act.wait_ge(o_ps, p + 1)
                        act.activation(sqbuf[:, :], ps[:, O_BANK, :], ACT.Square).then_inc(o_sq, 1)
                        if o >= 0:
                            act.wait_ge(y_ready, o + 1)
                        act.activation(acc[:, :], ps[:, O_BANK, :], ACT.Copy,
                                       scale=sub_gain[:, 0:1]).then_inc(o_taken, 1)
                root(head_ms, HEADS + 2, 4, 5, head_root)
                round_y(HEADS - 1)
                out_projection("even_out", 2, ahead=4)

            def round_y(o):
                act.wait_ge(o_scaled, o + 1)
                act.activation(h[:, Y0 + o, 0, :], acc[:, :], ACT.Copy).then_inc(y_hi, 1)

            def odd_mixer():
                r0 = start["odd"]

                def group(g, next_blocks=6, stats=False, following="odd"):
                    if stats:
                        round_unit(r0, 2, 6, phase="odd")
                        round_unit(r0, 3, 6, phase="odd")
                        root(norm_ms, 5, 0, 1, norm_root)
                    for slot in range(RING if following == "odd" else 2):
                        round_unit(r0 + g + 1, slot, next_blocks, phase=following)
                    act.wait_ge(cols_ready, 1)
                    act.wait_ge(conv_new, g + 1)
                    act.activation(h[:, Y0 + g, 0, :], obuf[:, :], ACT.Copy).then_inc(conv_hi, 1)

                group(0, stats=True)
                with act.Fori(1, NB - 1) as g:
                    group(g)
                group(NB - 1, next_blocks=NB, following="odd_out")
                out_projection("odd_out", 5, ahead=2)

            act.wait_ge(cols_ready, 1)
            for kind, m in FIRST_SPLITS:
                if kind == "unit":
                    round_unit(0, m, first=True)
                    continue
                act.wait_ge(x_new, m + 1)
                act.activation(gx[:, m, 0, :], x[:, m, :], ACT.Copy, scale=cols[:, m:m + 1]).then_inc(xhi_done, 1)
                if m >= 2:
                    act.wait_ge(sq_added, m - 1)
                act.activation(first_squares(m)[:, :], x[:, m, :], ACT.Square).then_inc(sq_done, 1)
            ffn(0)
            even_mixer()
            ffn(1)
            ffn(2)
            odd_mixer()
            ffn(3)

        @block.vector
        def _(dve):
            steps = [0]

            def then(instruction):
                steps[0] += 1
                instruction.then_inc(step, 1)
                dve.wait_ge(step, steps[0])

            def split_unit(rnd, slot, blocks=NB):
                dve.wait_ge(hi_done, RING * rnd + slot + 1)
                dve.tensor_tensor(wlo[:, slot, 0:blocks * P], raw[:, slot, 0:blocks * P],
                                  whi[:, slot, 0:blocks * P], ALU.subtract).then_inc(lo_done, 1)

            def rest_of_gx(phase, m):
                g = NB * phase + m
                dve.wait_ge(xhi_done, g + 1)
                dve.wait_ge(x_new, g + 1)
                dve.scalar_tensor_tensor(gx[:, m, 1, :], x[:, m, :], cols[:, bass.ds(g, 1)],
                                         gx[:, m, 0, :], ALU.mult, ALU.subtract).then_inc(gx_ready, 1)

            def residual(phase, m, bank, coefficient, ready, count):
                g = NB * phase + m
                dve.wait_ge(ready, count)
                dve.scalar_tensor_tensor(x[:, m, :], ps[:, bank, :], coefficient, x[:, m, :],
                                         ALU.mult, ALU.add).then_inc(x_new, 1)
                rest_of_gx(phase, m)
                dve.wait_ge(sq_done, g + 1)
                dve.wait_ge(sq_added, g)
                dve.tensor_tensor(acc[:, :], acc[:, :], sqbuf[:, :], ALU.add).then_inc(sq_added, 1)

            def clear_acc():
                then(dve.memset(acc[:, :], 0.0))

            def inverse_root(first, end, ms_done, root_done, count):
                a, b, c, d = (buf[:, :, first:end] for buf in (rs, nt, ms, sd))
                dve.wait_ge(ms_done, count)
                dve.wait_ge(root_done, count)
                then(dve.reciprocal(a, d))
                then(dve.tensor_tensor(b, a, a, ALU.mult))
                then(dve.tensor_tensor(b, b, c, ALU.mult))
                then(dve.tensor_scalar(b, b, -0.5, 1.5, ALU.mult, ALU.add))
                then(dve.tensor_tensor(a, a, b, ALU.mult))

            def diagonal(dst, factors):
                return dve.tensor_tensor(dst.rearrange("p (b n) -> p b n", b=TB),
                                         ident[:, :].unsqueeze(1).to_broadcast([P, TB, P]),
                                         factors.to_broadcast([P, TB, P]), ALU.mult)

            def norm_factors(r):
                dve.wait_ge(norm_stats, r + 1)
                dve.tensor_scalar(ms[:, :, 0:1], ps[:, STAT_BANK, 0:TB].unsqueeze(2), 1.0 / D, EPS,
                                  ALU.mult, ALU.add).then_inc(norm_ms, 1)
                inverse_root(0, 1, norm_ms, norm_root, r + 1)
                then(dve.tensor_copy(Rc[:, :].unsqueeze(2), rs[:, :, 0:1]))
                diagonal(obuf[:, :], Rc[:, :].unsqueeze(2)).then_inc(norm_diag, 1)

            def norm_rows(r):
                dve.wait_ge(norm_spread, r + 1)
                dve.tensor_copy(R[:, :], ps[:, SPREAD_BANK, :]).then_inc(norm_ready, 1)
                dve.wait_ge(norm_ready, r + 1)

            def ffn(f):
                phase = FFNS[f][4]
                r0 = start[f"ffn{f}"]
                r1 = r0 + FT // 2

                def hidden(t, s):
                    dve.wait_ge(w_used, RING * r0 + 2 * t + 2)
                    dve.tensor_tensor(gbuf[:, PAD:], ps[:, GATE_BANKS[s], :], R[:, :],
                                      ALU.mult).then_inc(gate_scaled, 1)
                    dve.wait_ge(h_ready, FT * f + t)
                    dve.tensor_tensor(ubuf[:, :], ps[:, GATE_BANKS[s] + 1, :], R[:, :],
                                      ALU.mult).then_inc(up_scaled, 1)
                    dve.wait_ge(silu_done, FT * f + t + 1)
                    dve.wait_ge(up_scaled, FT * f + t + 1)
                    dve.tensor_tensor(ubuf[:, :], gbuf[:, PAD:], ubuf[:, :], ALU.mult).then_inc(h_new, 1)
                    dve.wait_ge(hhi_done, FT * f + t + 1)
                    dve.tensor_tensor(h[:, t, 1, :], ubuf[:, :], h[:, t, 0, :],
                                      ALU.subtract).then_inc(h_ready, 1)

                def two_tiles(i):
                    split_unit(r0 + i, 2)
                    split_unit(r0 + i, 3)
                    hidden(2 * i, 0)
                    split_unit(r0 + i + 1, 0)
                    split_unit(r0 + i + 1, 1)
                    hidden(2 * i + 1, 1)

                norm_factors(phase - 1)
                if f:
                    split_unit(r0, 2)
                    split_unit(r0, 3)
                norm_rows(phase - 1)
                hidden(0, 0)
                split_unit(r0 + 1, 0)
                split_unit(r0 + 1, 1)
                hidden(1, 1)
                if f == 0:
                    dve.wait_ge(lam_in, 4 * 16)
                    then(dve.tensor_tensor(lam_prod[:, :, :], lam_rows[:, 0:2, :], lam_rows[:, 2:4, :],
                                           ALU.mult))
                    dve.reduce_sum(lam_sum[:, :], lam_prod[:, :, :], AX_X).then_inc(lam_sum_ready, 1)
                    dve.memset(lam_pair[:, 0:1], 1.0)
                    dve.wait_ge(lam_exp_ready, 1)
                    then(dve.tensor_tensor(lam_pair[:, 1:2], lam_exp[:, 1:2], lam_exp[:, 0:1], ALU.subtract))
                    then(dve.tensor_scalar(lam_pair[:, 1:2], lam_pair[:, 1:2], -LAM_INIT, None, ALU.add))
                with dve.Fori(1, FT // 2 - 1) as i:
                    two_tiles(i)
                split_unit(r1 - 1, 2)
                split_unit(r1 - 1, 3)
                hidden(FT - 2, 0)
                for s in range(RING):
                    split_unit(r1, s, DOWN_UNITS[s])
                hidden(FT - 1, 1)
                clear_acc()

                def next_tile(m):
                    for s in range(RING):
                        split_unit(r1 + m + 1, s, DOWN_UNITS[s])

                def down_result(m, s, first=False):
                    dve.wait_ge(w_used, units_used(r1 + m, RING - 1))
                    if not first:
                        dve.wait_ge(outT_ps, m - 1)
                    dve.scalar_tensor_tensor(fin(s)[:, :], ps[:, RES_BANKS[s], :], 0.5, x[:, m, :],
                                             ALU.mult, ALU.add).then_inc(fin_ready, 1)

                def down_residual(m, s):
                    residual(phase, m, RES_BANKS[s], 0.5, w_used, units_used(r1 + m, RING - 1))

                if f < 3:
                    with dve.Fori(0, NB // 2 - 1) as i:
                        for s in range(2):
                            next_tile(2 * i + s)
                            down_residual(2 * i + s, s)
                    next_tile(NB - 2)
                    down_residual(NB - 2, 0)
                    blocks = 6 if f == 2 else NB
                    split_unit(r1 + NB, 0, blocks)
                    split_unit(r1 + NB, 1, blocks)
                    down_residual(NB - 1, 1)
                else:
                    for m in range(2):
                        next_tile(m)
                        down_result(m, m, first=True)
                    with dve.Fori(1, NB // 2 - 1) as i:
                        for s in range(2):
                            next_tile(2 * i + s)
                            down_result(2 * i + s, s)
                    next_tile(NB - 2)
                    down_result(NB - 2, 0)
                    down_result(NB - 1, 1)

            def out_projection(name, phase, banks, ahead):
                def split_ahead(m):
                    if m + ahead < NB + 2:
                        split_unit(start[name] + (m + ahead) // RING, (m + ahead) % RING)

                for m in range(NB):
                    if ahead < RING:
                        split_ahead(m)
                    residual(phase, m, banks[m], 1.0, w_used, units_used(start[name], m))
                    if ahead == RING:
                        split_ahead(m)

            def row_maxima(hd, qb):
                n = (qb + 1) * P
                pair = ps[:, SCORE_BANKS[qb % 2]:SCORE_BANKS[qb % 2] + 2, :]
                dve.wait_ge(scores_ready, 4 * hd + qb + 1)
                then(dve.tensor_tensor(pair[:, :, n - P:n], pair[:, :, n - P:n],
                                       mask[:, :].unsqueeze(1).to_broadcast([P, 2, P]), ALU.add))
                then(dve.reduce_max(mx[:, qb % 2, :], pair[:, :, 0:n], AX_X))
                dve.tensor_tensor(nbias[:, qb % 2, :], mx[:, qb % 2, :], nqscale[:, qb, :],
                                  ALU.mult).then_inc(bias_ready, 1)

            def combine(hd, qb):
                n = (qb + 1) * P
                dve.wait_ge(exp_done, 4 * hd + qb + 1)
                then(dve.reciprocal(rec[:, qb % 2, :], sums[:, qb % 2, :]))
                then(dve.tensor_tensor(rec[:, qb % 2, :], rec[:, qb % 2, :], lam_pair[:, :], ALU.mult))
                then(dve.tensor_scalar(probs[:, qb % 2, 1, 0:n], probs[:, qb % 2, 1, 0:n],
                                       rec[:, qb % 2, 1:2], None, ALU.mult))
                dve.scalar_tensor_tensor(probs[:, qb % 2, 0, 0:n], probs[:, qb % 2, 0, 0:n],
                                         rec[:, qb % 2, 0:1], probs[:, qb % 2, 1, 0:n],
                                         ALU.mult, ALU.add).then_inc(w_ready, 1)

            def split_weights(hd, *qbs):
                dve.wait_ge(wt_hi, 4 * hd + qbs[-1] + 1)
                for qb in qbs:
                    at = P if qb == 1 else 0
                    last = dve.tensor_tensor(h[:, WT0:WT0 + qb + 1, 1, qb * P:(qb + 1) * P],
                                             ps[:, WT_BANKS[qb], at:at + (qb + 1) * P].rearrange(
                                                 "p (k n) -> p k n", n=P),
                                             h[:, WT0:WT0 + qb + 1, 0, qb * P:(qb + 1) * P], ALU.subtract)
                last.then_inc(wt_ready, len(qbs))

            def head_factors(stage, bank, c=None, o=None):
                dve.wait_ge(head_stats, stage + 1)
                if o is not None:
                    last = dve.tensor_scalar(ms[:, :, 4:5], ps[:, bank, 16:16 + TB].unsqueeze(2), 1.0 / P, EPS,
                                             ALU.mult, ALU.add)
                if c is not None:
                    then(dve.tensor_tensor(ms[:, :, 0:4], ps[:, bank, 0:16].rearrange("p (b c) -> p b c", b=TB),
                                           Rc2[:, :].unsqueeze(2).to_broadcast([P, TB, 4]), ALU.mult))
                    last = dve.tensor_scalar(ms[:, :, 0:4], ms[:, :, 0:4], 1.0 / HD, EPS, ALU.mult, ALU.add)
                last.then_inc(head_ms, 1)
                inverse_root(0 if c is not None else 4, 5 if o is not None else 4, head_ms, head_root, stage + 1)
                if c is not None:
                    then(dve.tensor_tensor(rs[:, :, 0:4], rs[:, :, 0:4],
                                           Rc[:, :].unsqueeze(2).to_broadcast([P, TB, 4]), ALU.mult))
                    for j in range(2):
                        last = diagonal(sq_qk[:, j, :], rs[:, :, 2 + j:3 + j])
                    last.then_inc(qk_diag, 1)
                if o is not None:
                    diagonal(obuf[:, :], rs[:, :, 4:5]).then_inc(o_diag, 1)
                if c is not None:
                    dve.tensor_scalar(qscale[:, :, :], rs[:, :, 0:2], HD ** -0.5, None, ALU.mult)
                    then(dve.tensor_scalar(nqscale[:, :, :], rs[:, :, 0:2], -HD ** -0.5, None, ALU.mult))

            def scale_o(o):
                dve.wait_ge(o_taken, o + 1)
                dve.wait_ge(o_spread, o + 1)
                dve.tensor_tensor(acc[:, :], acc[:, :], ps[:, O_SPREAD_BANK, :], ALU.mult).then_inc(o_scaled, 1)

            def rest_of_y(o):
                dve.wait_ge(y_hi, o + 1)
                dve.wait_ge(o_scaled, o + 1)
                dve.tensor_tensor(h[:, Y0 + o, 1, :], acc[:, :], h[:, Y0 + o, 0, :],
                                  ALU.subtract).then_inc(y_ready, 1)

            def even_mixer():
                r0 = start["even"]
                split_unit(r0, 2)
                split_unit(r0, 3)
                split_unit(r0 + 1, 0)
                split_unit(r0 + 1, 1)
                norm_factors(1)
                then(dve.tensor_tensor(Rc2[:, :], Rc[:, :], Rc[:, :], ALU.mult))
                for tb in range(TB):
                    dve.wait_ge(v_hi, tb + 1)
                    dve.scalar_tensor_tensor(h[:, V0 + tb, 1, :], ps[:, V_BANK + tb, :], Rc[:, tb:tb + 1],
                                             h[:, V0 + tb, 0, :], ALU.mult, ALU.subtract).then_inc(v_ready, 1)
                for c in range(HEADS + 1):
                    p, o = c - 1, c - 2
                    if p >= 0:
                        row_maxima(p, 0)
                        row_maxima(p, 1)
                        combine(p, 0)
                        combine(p, 1)
                    if c < HEADS:
                        dve.wait_ge(q_hi, c + 1)
                        dve.scalar_tensor_tensor(h[:, Q0 + c % 2, 1, :], ps[:, Q_BANK, :],
                                                 cols[:, COL_QGAIN:COL_QGAIN + 1], h[:, Q0 + c % 2, 0, :],
                                                 ALU.mult, ALU.subtract).then_inc(q_taken, 1)
                    if c == 0:
                        norm_rows(1)
                        dve.wait_ge(wpool_hi, 1)
                        dve.tensor_tensor(h[:, WPOOL, 1, :], acc[:, :], h[:, WPOOL, 0, :],
                                          ALU.subtract).then_inc(wpool_ready, 1)
                    if p >= 0:
                        split_weights(p, 0, 1)
                        row_maxima(p, 2)
                        row_maxima(p, 3)
                        combine(p, 2)
                        combine(p, 3)
                        split_weights(p, 2)
                        split_weights(p, 3)
                    head_factors(c, HEAD_STAT_BANK, c=c if c < HEADS else None, o=o if o >= 0 else None)
                    if c < HEADS:
                        dve.wait_ge(w_used, units_used(r0 + 1, 3 * c + 2))
                        if c:
                            dve.wait_ge(pooled_new, c)
                        dve.tensor_tensor(tbuf[:, PAD:], ps[:, U_BANK, :], R[:, :], ALU.mult).then_inc(u_taken, 1)
                        dve.wait_ge(k_taken, c + 1)
                        dve.wait_ge(qk_spread, c + 1)
                        dve.tensor_tensor(ubuf[:, :], ubuf[:, :], ps[:, K_SPREAD_BANK, :],
                                          ALU.mult).then_inc(k_scaled, 1)
                    if o >= 0:
                        scale_o(o)
                    if c < HEADS:
                        dve.wait_ge(k_hi, c + 1)
                        dve.tensor_tensor(h[:, K0, 1, :], ubuf[:, :], h[:, K0, 0, :],
                                          ALU.subtract).then_inc(k_ready, 1)
                    if o >= 0:
                        rest_of_y(o)
                    if p >= 0:
                        dve.wait_ge(pool_hi, p + 1)
                        dve.scalar_tensor_tensor(h[:, Y0 + HEADS + p, 1, :], ps[:, POOL_BANK, :],
                                                 cols[:, COL_PSCALE + p:COL_PSCALE + p + 1],
                                                 h[:, Y0 + HEADS + p, 0, :],
                                                 ALU.mult, ALU.subtract).then_inc(pool_ready, 1)
                head_factors(HEADS + 1, O_STAT_BANK, o=HEADS - 1)
                scale_o(HEADS - 1)
                rest_of_y(HEADS - 1)
                dve.wait_ge(y_ready, HEADS)
                clear_acc()
                dve.wait_ge(lo_done, RING * (start["even_out"] + 1))
                out_projection("even_out", 2, EVEN_TILE_BANKS, ahead=RING)

            def odd_mixer():
                r0 = start["odd"]

                def group(g, s, next_blocks=6, stats=False, more=True):
                    banks = GROUP_BANKS[s]
                    if stats:
                        split_unit(r0, 2, 6)
                        split_unit(r0, 3, 6)
                        norm_factors(4)
                    split_unit(r0 + g + 1, 0, next_blocks)
                    split_unit(r0 + g + 1, 1, next_blocks)
                    if stats:
                        norm_rows(4)
                    dve.wait_ge(w_used, units_used(r0 + g, RING - 1))
                    dve.tensor_tensor(gbuf[:, PAD:], ps[:, banks[1], :], R[:, :], ALU.mult)
                    dve.tensor_tensor(ubuf[:, :], ps[:, banks[2], :], R[:, :], ALU.mult).then_inc(conv_step, 1)
                    dve.tensor_tensor(obuf[:, :], ps[:, banks[0], :], R[:, :], ALU.mult).then_inc(group_taken, 1)
                    dve.wait_ge(conv_step, 5 * g + 1)
                    dve.tensor_tensor(zbuf[:, PAD:], gbuf[:, PAD:], ubuf[:, :], ALU.mult).then_inc(conv_step, 1)
                    dve.wait_ge(conv_step, 5 * g + 2)
                    if more:
                        split_unit(r0 + g + 1, 2, 6)
                    for j in range(CONV):
                        shifted = zbuf[:, PAD - (CONV - 1 - j):PAD - (CONV - 1 - j) + T]
                        tap = cols[:, bass.ds(g + (COL_CONV + NB * j), 1)]
                        if j == 0:
                            dve.tensor_scalar(sqbuf[:, :], shifted, tap, None, ALU.mult).then_inc(conv_step, 1)
                        else:
                            dve.scalar_tensor_tensor(sqbuf[:, :], shifted, tap, sqbuf[:, :], ALU.mult,
                                                     ALU.add).then_inc(conv_step, 1)
                        dve.wait_ge(conv_step, 5 * g + 3 + j)
                    dve.tensor_tensor(obuf[:, :], obuf[:, :], sqbuf[:, :], ALU.mult).then_inc(conv_new, 1)
                    dve.wait_ge(conv_hi, g + 1)
                    dve.tensor_tensor(h[:, Y0 + g, 1, :], obuf[:, :], h[:, Y0 + g, 0, :],
                                      ALU.subtract).then_inc(conv_ready, 1)
                    if more:
                        split_unit(r0 + g + 1, 3, 6)

                group(0, 0, stats=True)
                group(1, 1)
                with dve.Fori(1, NB // 2 - 1) as i:
                    group(2 * i, 0)
                    group(2 * i + 1, 1)
                group(NB - 2, 0)
                group(NB - 1, 1, next_blocks=NB, more=False)
                clear_acc()
                out_projection("odd_out", 5, RES_BANKS * (NB // 2), ahead=2)

            dve.wait_ge(cols_ps, 1)
            dve.tensor_copy(cols[:, 0:NB], ps[:, SPREAD_BANK, 0:NB]).then_inc(cols_ready, 1)

            def copy_block(m):
                dve.wait_ge(xT_ps, m + 1)
                dve.tensor_copy(x[:, m, :], ps[:, m, :]).then_inc(x_new, 1)

            copy_block(0)
            copy_block(1)
            for kind, m in FIRST_SPLITS:
                if kind == "unit":
                    split_unit(0, m)
                    continue
                if m + 2 < NB:
                    copy_block(m + 2)
                rest_of_gx(0, m)
            dve.wait_ge(cols_ps, 2)
            dve.tensor_copy(cols[:, NB:N_COLS], ps[:, SPREAD_BANK, NB:N_COLS]).then_inc(cols_ready, 1)
            dve.wait_ge(cols_ready, 2)
            dve.tensor_scalar(sub_gain[:, :], cols[:, COL_SUB:COL_SUB + 1], 1.0 - LAM_INIT, None, ALU.mult)
            ffn(0)
            even_mixer()
            ffn(1)
            ffn(2)
            odd_mixer()
            ffn(3)


_INS = ["x", "ffn1_norm", "ffn1_w_gate", "ffn1_w_up", "ffn1_w_down", "ffn2_norm", "ffn2_w_gate", "ffn2_w_up",
        "ffn2_w_down", "mix_norm", "even_w_in", "even_w_out", "q_gain", "k_gain", "subln_gain", "lambda_q1",
        "lambda_k1", "lambda_q2", "lambda_k2", "w_pool", "pool_scale", "odd_w_in", "conv_w", "odd_w_out"]
_OUT = ((1, T, D), "float32")


def kernel(**inputs):
    import numpy as _np
    import concourse.bacc as _bacc
    from concourse import mybir as _mybir
    from concourse.bass_utils import run_bass_kernel_spmd as _run

    nc = _bacc.Bacc("TRN2", target_bir_lowering=False, num_devices=1,
                    dynamic_dma_scratch_size=2048)
    arrays, args = {}, []
    for name in _INS:
        a = _np.ascontiguousarray(inputs[name])
        arrays[f"in_{name}"] = a
        args.append(nc.dram_tensor(f"in_{name}", a.shape, _mybir.dt.from_np(a.dtype), kind="ExternalInput").ap())
    shape, dtype = _OUT
    out = nc.dram_tensor("out", shape, _mybir.dt.from_np(_np.dtype(dtype)), kind="ExternalOutput").ap()
    build(nc, *args, out)
    r = _run(nc, [arrays], core_ids=[0])
    return r.results[0]["out"]
```

```python
from contextlib import ExitStack

import concourse.bass as bass
from concourse import mybir

F32 = mybir.dt.float32
F32R = mybir.dt.float32r
ALU = mybir.AluOpType
ACT = mybir.ActivationFunctionType
AX_X = mybir.AxisListType.X

P = 128
D = 1024
T = 512
FF = 2816
NB = D // P
TB = T // P
FT = FF // P
HEADS = 4
HD = 64
WINDOWS = (2, 4, 8, 16)
CONV = 3
EPS = 1e-6
LAM_INIT = 0.8 - 0.6
MASKED = -1e30
RING = 4
UNIT = 8 * P
PAD = 8

DOWN_UNITS = (6, 6, 5, 5)
DOWN_FIRST = (0, 6, 12, 17)


GATE_BANKS = (0, 2)
RES_BANKS = (4, 5)
GROUP_BANKS = ((0, 1, 2), (3, 6, 7))
STAT_BANK = 6
SPREAD_BANK = 7
Q_BANK = U_BANK = 0
K_BANK = 1
V_BANK = 2
SCORE_BANKS = (2, 4)
WT_BANKS = (6, 6, 7, 6)
HEAD_STAT_BANK = 2
K_SPREAD_BANK = 3
O_SPREAD_BANK = 4
POOL_BANK = 5
O_BANK = 7
O_STAT_BANK = 6
EVEN_TILE_BANKS = (0, 1, 3, 2, 4, 5, 6, 7)
OUT_BANKS = (6, 7)

WT0, Y0, V0, Q0, K0, POOLED, WPOOL = 1, 5, 13, 17, 19, 20, 21
NORM_ROWS = 6 * NB
COL_CONV = NORM_ROWS
COL_PSCALE = COL_CONV + CONV * NB
COL_QGAIN = COL_PSCALE + HEADS
COL_KGAIN, COL_SUB, N_COLS = COL_QGAIN + 1, COL_QGAIN + 2, COL_QGAIN + 3


def build(nc, x_in, ffn1_norm, ffn1_w_gate, ffn1_w_up, ffn1_w_down, ffn2_norm, ffn2_w_gate,
          ffn2_w_up, ffn2_w_down, mix_norm, even_w_in, even_w_out, q_gain, k_gain, subln_gain,
          lambda_q1, lambda_k1, lambda_q2, lambda_k2, w_pool, pool_scale, odd_w_in, conv_w,
          odd_w_out, out):
    start, rounds = {}, 0
    for name, units in (("ffn0", 2 * FT + 4 * NB), ("even", 4 + 3 * HEADS), ("even_out", NB),
                        ("ffn1", 2 * FT + 4 * NB), ("ffn2", 2 * FT + 4 * NB), ("odd", 4 * NB),
                        ("odd_out", NB), ("ffn3", 2 * FT + 4 * NB)):
        assert units % RING == 0
        start[name] = rounds
        rounds += units // RING
    FFNS = ((ffn1_w_gate, ffn1_w_up, ffn1_w_down, 0, 1), (ffn2_w_gate, ffn2_w_up, ffn2_w_down, 0, 3),
            (ffn1_w_gate, ffn1_w_up, ffn1_w_down, 1, 4), (ffn2_w_gate, ffn2_w_up, ffn2_w_down, 1, 6))

    with ExitStack() as ctx:
        def sb(name, shape, dt=F32):
            return ctx.enter_context(nc.sbuf_tensor(name, shape, dt))

        def sem(name):
            return ctx.enter_context(nc.semaphore(name))

        with nc.sbuf_tensor("x_tok", [P, TB, D], F32) as x_tok:
            pass
        with nc.sbuf_tensor("sq_qk", [P, 2, T], F32) as sq_qk:
            pass
        h = sb("h", [P, FT, 2, T], F32R)
        x = sb("x", [P, NB, T])
        gx = sb("gx", [P, NB, 2, T], F32R)
        raw = sb("raw", [P, RING, UNIT])
        whi = sb("whi", [P, RING, UNIT], F32R)
        wlo = sb("wlo", [P, RING, UNIT], F32R)
        R = sb("R", [P, T])
        acc = sb("acc", [P, T])
        gbuf = sb("gbuf", [P, PAD + T])
        zbuf = sb("zbuf", [P, PAD + T])
        ubuf = sb("ubuf", [P, T])
        tbuf = sb("tbuf", [P, PAD + T])
        sqbuf = sb("sqbuf", [P, T])
        obuf = sb("obuf", [P, T])
        probs = sb("probs", [P, 2, 2, T])
        ident = sb("ident", [P, P])
        ones = sb("ones", [P, P])
        ones_r = sb("ones_r", [P, P], F32R)
        mask = sb("mask", [P, P])
        halves = sb("halves", [P, 2])
        rows = sb("rows", [N_COLS, P])
        cols = sb("cols", [P, N_COLS])
        counts = sb("counts", [P, 16])
        ms = sb("ms", [P, TB, 5])
        sd = sb("sd", [P, TB, 5])
        rs = sb("rs", [P, TB, 5])
        nt = sb("nt", [P, TB, 5])
        Rc = sb("Rc", [P, TB])
        Rc2 = sb("Rc2", [P, TB])
        qscale = sb("qscale", [P, TB, 2])
        nqscale = sb("nqscale", [P, TB, 2])
        mx = sb("mx", [P, 2, 2])
        nbias = sb("nbias", [P, 2, 2])
        sums = sb("sums", [P, 2, 2])
        rec = sb("rec", [P, 2, 2])
        lam_rows = sb("lam_rows", [P, 4, HD])
        lam_prod = sb("lam_prod", [P, 2, HD])
        lam_sum = sb("lam_sum", [P, 2])
        lam_exp = sb("lam_exp", [P, 2])
        lam_pair = sb("lam_pair", [P, 2])
        sub_gain = sb("sub_gain", [P, 1])
        ps = ctx.enter_context(nc.psum_tensor("ps", [P, 8, T], F32))

        raw_in = [sem(f"raw_in{i}") for i in range(RING)]
        x_loaded = [sem(f"x_loaded{i}") for i in range(TB)]
        stored = [sem(f"stored{i}") for i in range(2)]
        (first_gains_in, params_in, lam_in, wpool_in, consts, cols_ps, cols_ready, lam_sum_ready, lam_exp_ready,
         hi_done, lo_done, w_used, xT_ps, x_new, xhi_done, sq_done, sq_added, gx_ready,
         acc_hi, acc_lo, norm_stats, norm_ms, norm_root, norm_diag, norm_spread, norm_ready,
         gate_scaled, up_scaled, silu_done, h_new, hhi_done, h_ready,
         v_hi, v_ready, q_hi, q_sq, q_taken, k_sq, k_taken, u_taken,
         head_stats, head_ms, head_root, qk_diag, qk_spread, k_scaled, k_hi, k_ready,
         scores_ready, bias_ready, exp_done, w_ready, wt_ps, wt_hi, wt_ready,
         o_ps, o_sq, o_taken, o_diag, o_spread, o_scaled, y_hi, y_ready,
         wpool_hi, wpool_ready, pooled_new, pooled_hi, pooled_ready, pool_ps, pool_hi, pool_ready,
         group_taken, acc_zero, window_step, conv_step, conv_new, conv_hi, conv_ready, fin_ready, outT_ps,
         outT_copied, step) = [
            sem(name) for name in (
                "first_gains_in params_in lam_in wpool_in consts cols_ps cols_ready lam_sum_ready lam_exp_ready "
                "hi_done lo_done w_used xT_ps x_new xhi_done sq_done sq_added gx_ready "
                "acc_hi acc_lo norm_stats norm_ms norm_root norm_diag norm_spread norm_ready "
                "gate_scaled up_scaled silu_done h_new hhi_done h_ready "
                "v_hi v_ready q_hi q_sq q_taken k_sq k_taken u_taken "
                "head_stats head_ms head_root qk_diag qk_spread k_scaled k_hi k_ready "
                "scores_ready bias_ready exp_done w_ready wt_ps wt_hi wt_ready "
                "o_ps o_sq o_taken o_diag o_spread o_scaled y_hi y_ready "
                "wpool_hi wpool_ready pooled_new pooled_hi pooled_ready pool_ps pool_hi pool_ready "
                "group_taken acc_zero window_step conv_step conv_new conv_hi conv_ready fin_ready outT_ps "
                "outT_copied step").split()]
        FIRST_STEPS = (("x", 0), ("unit", 0), ("square", 0), ("x", 1), ("square", 1), ("x", 2), ("square", 2),
                       ("x", 3), ("square", 3), ("unit", 1), ("unit", 2), ("x", 4), ("square", 4), ("unit", 3),
                       ("x", 5), ("square", 5), ("x", 6), ("square", 6), ("x", 7), ("square", 7))
        N_CONSTS = 12
        N_PARAMS = 10

        def loaded(rnd, phase):
            if phase == "odd":
                return 32 * (rnd + 1) + -16 * start["odd"]
            return 16 * (rnd + 1) + (16 * NB if phase in ("odd_out", "ffn3") else 0)

        def units_used(rnd, slot):
            return RING * rnd + slot + 1

        def spread_cols(src):
            return src.unsqueeze(2).to_broadcast([P, TB, P])

        def squares(m):
            return (sqbuf, obuf)[m % 2]

        def wide_norms(r):
            return r + 1 - (r >= 1)

        def fin(s):
            return (sqbuf, obuf)[s]

        def pooled(g):
            return (gbuf, zbuf)[g % 2][:, PAD:]

        block = ctx.enter_context(nc.Block())

        @block.sync
        def _(sp):
            def load(rnd, slot, *parts, first=False):
                if not first:
                    sp.wait_ge(lo_done, RING * (rnd - 1) + slot + 1)
                at = 0
                for src in parts:
                    _, blocks, n = src.shape
                    sp.dma_start(raw[:, slot, at:at + blocks * n].rearrange("p (a n) -> p a n", a=blocks),
                                 src).then_inc(raw_in[slot], 16)
                    at += blocks * n

            def columns(w, col, first_block=0, blocks=NB, width=P):
                return w.rearrange("(c p) n -> p c n", p=P)[:, first_block:first_block + blocks,
                                                            bass.ds(col, width)]

            def row_load(row, src, loads):
                sp.dma_start(rows[row:row + src.shape[0], :], src).then_inc(loads, 16)

            def parameters():
                for r, src in ((1, mix_norm[0]), (2, ffn2_norm[0]), (3, ffn1_norm[1]), (4, mix_norm[1]),
                               (5, ffn2_norm[1])):
                    row_load(NB * r, src.rearrange("(c p) -> c p", p=P), params_in)
                row_load(COL_CONV, conv_w[0].rearrange("j (c p) -> (j c) p", p=P), params_in)
                row_load(COL_PSCALE, pool_scale[0].rearrange("(c p) -> c p", p=P), params_in)
                for row, src in ((COL_QGAIN, q_gain), (COL_KGAIN, k_gain)):
                    sp.dma_start(rows[row:row + 1, :].rearrange("a (c p) -> a c p", c=2),
                                 src.unsqueeze(1).to_broadcast([1, 2, HD])).then_inc(params_in, 16)
                row_load(COL_SUB, subln_gain, params_in)
                for j, src in enumerate((lambda_q1, lambda_q2, lambda_k1, lambda_k2)):
                    sp.dma_start(lam_rows[:, j, :], src.to_broadcast([P, HD])).then_inc(lam_in, 16)

            def ffn(f):
                w_gate, w_up, w_down, layer, _ = FFNS[f]
                r0 = start[f"ffn{f}"]
                r1 = r0 + FT // 2

                def two_tiles(i):
                    for s in range(2):
                        load(r0 + i, 2 * s, columns(w_gate[layer], (2 * i + s) * P))
                        load(r0 + i, 2 * s + 1, columns(w_up[layer], (2 * i + s) * P))

                with sp.Fori(1 if f == 0 else 0, FT // 2) as i:
                    two_tiles(i)
                with sp.Fori(0, NB) as m:
                    for s in range(RING):
                        load(r1 + m, s, columns(w_down[layer], m * P, DOWN_FIRST[s], DOWN_UNITS[s]))

            def out_projection(name, w):
                with sp.Fori(0, NB // RING) as i:
                    for s in range(RING):
                        load(start[name] + i, s, columns(w, (RING * i + s) * P))

            row_load(0, ffn1_norm[0].rearrange("(c p) -> c p", p=P), first_gains_in)

            def x_half(half):
                channels = slice(half * D // 2, (half + 1) * D // 2)
                for pair in range(2):
                    sp.dma_start(x_tok[:, 2 * pair:2 * pair + 2, channels],
                                 x_in[0].rearrange("(b p) d -> p b d", p=P)[:, 2 * pair:2 * pair + 2, channels]
                                 ).then_inc(x_loaded[2 * half + pair], 16)

            def first_unit(slot):
                load(0, slot, columns((ffn1_w_gate, ffn1_w_up)[slot % 2][0], slot // 2 * P), first=True)

            x_half(0)
            first_unit(0)
            x_half(1)
            for slot in range(1, RING):
                first_unit(slot)
            parameters()
            ffn(0)
            r0 = start["even"]
            for s in range(RING):
                load(r0, s, columns(even_w_in[0], 2 * T, 2 * s, 2, T))
            for n in range(3 * HEADS):
                head, kind = divmod(n, 3)
                load(r0 + 1 + n // RING, n % RING, columns(even_w_in[0], (0, T, 3 * T)[kind] + head * P))
                if n == 2:
                    sp.wait_ge(norm_ms, 2)
                    sp.dma_start(acc[:, :].rearrange("p (g d) -> p g d", g=HEADS),
                                 w_pool[0].rearrange("g c d -> c g d")).then_inc(wpool_in, 16)
            out_projection("even_out", even_w_out[0])
            ffn(1)
            ffn(2)
            w_bch = odd_w_in[0].rearrange("(c p) (k n) -> p c k n", p=P, k=3)
            with sp.Fori(0, NB) as g:
                for s in range(RING):
                    load(start["odd"] + g, s, *(w_bch[:, 2 * s + j, :, bass.ds(g * P, P)] for j in range(2)))
            out_projection("odd_out", odd_w_out[0])
            ffn(3)
            for s in range(2):
                sp.wait_ge(stored[s], 16 * (NB // 2))

        @block.gpsimd
        def _(pool):
            pool.memset(ones[:, :], 1.0).then_inc(consts, 1)
            pool.memset(ident[:, :], 0.0).then_inc(consts, 1)
            pool.memset(mask[:, :], 0.0).then_inc(consts, 1)
            pool.memset(halves[:, :], 0.0).then_inc(consts, 1)
            pool.memset(gbuf[:, 0:PAD], 0.0).then_inc(consts, 1)
            pool.memset(zbuf[:, 0:PAD], 0.0).then_inc(consts, 1)
            pool.memset(tbuf[:, 0:PAD], 0.0).then_inc(consts, 1)
            pool.wait_ge(consts, 7)
            pool.affine_select(out=ident[:, :], in_=ident[:, :], compare_op=ALU.not_equal, fill=1.0,
                               base=0, pattern=[[-1, P]], channel_multiplier=1).then_inc(consts, 1)
            pool.affine_select(out=mask[:, :], in_=mask[:, :], compare_op=ALU.is_ge, fill=MASKED,
                               base=0, pattern=[[-1, P]], channel_multiplier=1).then_inc(consts, 1)
            pool.wait_ge(consts, 9)
            pool.memset(halves[0:HD, 0:1], 1.0).then_inc(consts, 1)
            pool.wait_ge(consts, 10)
            pool.memset(halves[HD:P, 1:2], 1.0).then_inc(consts, 1)
            pool.wait_ge(consts, 11)
            for t in range(max(WINDOWS)):
                last = pool.memset(counts[:, t:t + 1], 1.0 / (t + 1))
            last.then_inc(consts, 1)
            pool.memset(acc[:, :], 0.0).then_inc(acc_zero, 1)
            pool.wait_ge(acc_zero, 1)
            for m in range(NB):
                pool.wait_ge(sq_done, m + 1)
                pool.tensor_tensor(acc[:, :], acc[:, :], squares(m)[:, :], ALU.add).then_inc(sq_added, 1)
                pool.wait_ge(sq_added, m + 1)

            steps = [0]

            def then(instruction):
                steps[0] += 1
                instruction.then_inc(window_step, 1)
                pool.wait_ge(window_step, steps[0])

            def pool_windows(g):
                w = WINDOWS[g]
                pool.wait_ge(u_taken, g + 1)
                if g:
                    pool.wait_ge(pooled_ready, g)
                src = tbuf
                for j in range(g + 1):
                    shift, dst = 2 ** j, (gbuf, zbuf)[j % 2]
                    then(pool.tensor_tensor(dst[:, PAD:], src[:, PAD:], src[:, PAD - shift:PAD + T - shift],
                                            ALU.add))
                    src = dst
                mean = pooled(g)
                then(pool.tensor_tensor(mean[:, 0:w], mean[:, 0:w], counts[:, 0:w], ALU.mult))
                then(pool.tensor_scalar(mean[:, w:], mean[:, w:], 1.0 / w, None, ALU.mult))
                pool.tensor_tensor(mean, mean, tbuf[:, PAD:], ALU.subtract).then_inc(pooled_new, 1)
                pool.wait_ge(pooled_hi, g + 1)
                pool.tensor_tensor(h[:, POOLED, 1, :], mean, h[:, POOLED, 0, :],
                                   ALU.subtract).then_inc(pooled_ready, 1)

            def split_units(first, end):
                for n in range(first, end):
                    slot = n % RING
                    pool.wait_ge(hi_done, RING * (start["even"] + 1) + n + 1)
                    pool.wait_ge(lo_done, RING * (start["even"] + 1) + n)
                    pool.tensor_tensor(wlo[:, slot, :], raw[:, slot, :], whi[:, slot, :],
                                       ALU.subtract).then_inc(lo_done, 1)

            for c in range(HEADS):
                if c:
                    pool_windows(c - 1)
                split_units(3 * c + 2, 3 * c + 5)
            pool_windows(HEADS - 1)

        @block.tensor
        def _(pe):
            def product(dst, lhs, rhs, begin, end):
                pe.matmul(dst, lhs[0], rhs[0], start=begin, stop=False)
                pe.matmul(dst, lhs[0], rhs[1], start=False, stop=False)
                return pe.matmul(dst, lhs[1], rhs[0], start=False, stop=end)

            def weight(slot, i, n=P):
                return whi[:, slot, i * n:(i + 1) * n], wlo[:, slot, i * n:(i + 1) * n]

            def gxb(k, a=0, b=T):
                return gx[:, k, 0, a:b], gx[:, k, 1, a:b]

            def hb(k, a=0, b=T, p0=0, p1=P):
                return h[p0:p1, k, 0, a:b], h[p0:p1, k, 1, a:b]

            def column_block(rnd, slot, bank, norm=None):
                pe.wait_ge(lo_done, RING * rnd + slot + 1)
                for k in range(NB):
                    if norm is not None:
                        pe.wait_ge(gx_ready, NB * norm + k + 1)
                    last = product(ps[:, bank, :], weight(slot, k), gxb(k), k == 0, k == NB - 1)
                last.then_inc(w_used, 1)

            def part_column_block(rnd, slot, bank, first, end):
                pe.wait_ge(lo_done, RING * rnd + slot + 1)
                for k in range(first, end):
                    last = product(ps[:, bank, :], weight(slot, k), gxb(k), k == 0, k == NB - 1)
                if end == NB:
                    last.then_inc(w_used, 1)

            def sum_of_norm(r):
                pe.wait_ge(acc_lo, wide_norms(r))
                pe.matmul(ps[:, SPREAD_BANK, :], ones_r[:, :], h[:, 0, 0, :], start=True, stop=False)
                pe.matmul(ps[:, SPREAD_BANK, :], ones_r[:, :], h[:, 0, 1, :], start=False,
                          stop=True).then_inc(norm_spread, 1)

            def mixer_norm_stats():
                pe.wait_ge(sq_added, 2 * NB)
                for tb in range(TB):
                    last = pe.matmul(ps[:, STAT_BANK, tb:tb + 1], acc[:, tb * P:(tb + 1) * P], ones[:, 0:1],
                                     start=True, stop=True)
                last.then_inc(norm_stats, 1)

            def mixer_norm_spread():
                pe.wait_ge(norm_diag, 1)
                pe.matmul(ps[:, SPREAD_BANK, :], ones[:, :], obuf[:, :], start=True,
                          stop=True).then_inc(norm_spread, 1)

            def transpose_x(half):
                for pair in range(2):
                    pe.wait_ge(x_loaded[2 * half + pair], 16)
                    for m in range(half * NB // 2, (half + 1) * NB // 2):
                        if pair == 0 and m == SPREAD_BANK:
                            pe.wait_ge(cols_ready, 1)
                        for tb in range(2 * pair, 2 * pair + 2):
                            last = pe.transpose(ps[:, m, tb * P:(tb + 1) * P],
                                                x_tok[:, tb, m * P:(m + 1) * P], ident[:, :])
                        if pair == 1:
                            last.then_inc(xT_ps, 1)

            def transpose_result(m, s, first=False):
                pe.wait_ge(fin_ready, m + 1)
                if not first:
                    pe.wait_ge(outT_copied, m - 1)
                for tb in range(TB):
                    last = pe.transpose(ps[:, OUT_BANKS[s], tb * P:(tb + 1) * P],
                                        fin(s)[:, tb * P:(tb + 1) * P], ident[:, :])
                last.then_inc(outT_ps, 1)

            def ffn(f):
                phase = FFNS[f][4]
                r0 = start[f"ffn{f}"]
                r1 = r0 + FT // 2

                def two_tiles(i, first=False):
                    for s in range(2):
                        new = first and s == 0
                        if not first:
                            pe.wait_ge(up_scaled, FT * f + 2 * i + s - 1)
                        column_block(r0 + i, 2 * s, GATE_BANKS[s], phase - 1 if new else None)
                        if new:
                            sum_of_norm(phase - 1)
                        column_block(r0 + i, 2 * s + 1, GATE_BANKS[s] + 1)

                def first_tiles():
                    for part in range(2):
                        for n in range(RING):
                            if part == 0:
                                pe.wait_ge(lo_done, n + 1)
                            for k in range(part * NB // 2, (part + 1) * NB // 2):
                                if n == 0:
                                    pe.wait_ge(gx_ready, k + 1)
                                last = product(ps[:, n, :], weight(n, k), gxb(k), k == 0, k == NB - 1)
                                if n == 0 and k == NB - 3:
                                    pe.wait_ge(cols_ready, 2)
                                    sum_of_norm(0)
                            if part == 0 and n == 0:
                                transpose_x(1)
                            if part == 1:
                                last.then_inc(w_used, 1)
                            if part == 0 and n == RING - 1:
                                pe.wait_ge(consts, N_CONSTS)
                                pe.wait_ge(params_in, 16 * N_PARAMS)
                                pe.wait_ge(x_new, NB)
                                pe.transpose(ps[:, SPREAD_BANK, 0:N_COLS], rows[:, :],
                                             ident[0:N_COLS, 0:N_COLS]).then_inc(cols_ps, 1)

                def down_tile(m, s, first=False):
                    for q in range(RING):
                        pe.wait_ge(lo_done, RING * (r1 + m) + q + 1)
                        for j in range(DOWN_UNITS[q]):
                            k = DOWN_FIRST[q] + j
                            if first and k == FT - 1:
                                pe.wait_ge(h_ready, FT * (f + 1))
                            last = product(ps[:, RES_BANKS[s], :], weight(q, j), hb(k), k == 0, k == FT - 1)
                        last.then_inc(w_used, 1)

                if f == 0:
                    first_tiles()
                else:
                    two_tiles(0, first=True)
                with pe.Fori(1, FT // 2) as i:
                    two_tiles(i)
                pe.wait_ge(h_ready, FT * (f + 1) - 1)
                if f < 3:
                    pe.wait_ge(x_new, NB * phase - 1)
                    down_tile(0, 0, first=True)
                    pe.wait_ge(x_new, NB * phase)
                    down_tile(1, 1)
                    with pe.Fori(1, NB // 2) as i:
                        for s in range(2):
                            m = 2 * i + s
                            pe.wait_ge(x_new, NB * phase + m - 1)
                            down_tile(m, s)
                else:
                    down_tile(0, 0, first=True)
                    down_tile(1, 1)
                    for s in range(2):
                        transpose_result(s, s, first=True)
                        down_tile(2 + s, s)
                    with pe.Fori(2, NB // 2) as i:
                        for s in range(2):
                            m = 2 * i + s
                            transpose_result(m - 2, s)
                            down_tile(m, s)
                    transpose_result(NB - 2, 0)
                    transpose_result(NB - 1, 1)

            def output_part(name, m, bank, blocks, end=False):
                for k in blocks:
                    last = product(ps[:, bank, :], weight(m % RING, k), hb(Y0 + k), k == HEADS,
                                   end and k == blocks[-1])
                if end:
                    last.then_inc(w_used, 1)

            def output_split(name, m):
                pe.wait_ge(lo_done, RING * start[name] + m + 1)

            def scores(hd, qb):
                if qb >= 2:
                    pe.wait_ge(exp_done, 4 * hd + qb - 1)
                for c in range(2):
                    p0, p1 = c * HD, (c + 1) * HD
                    last = product(ps[:, SCORE_BANKS[qb % 2] + c, 0:(qb + 1) * P],
                                   hb(Q0 + hd % 2, qb * P, (qb + 1) * P, p0, p1),
                                   hb(K0, 0, (qb + 1) * P, p0, p1), True, True)
                last.then_inc(scores_ready, 1)

            def transpose_weights(hd, *qbs):
                for qb in qbs:
                    pe.wait_ge(w_ready, 4 * hd + qb + 1)
                    at = P if qb == 1 else 0
                    for kb in range(qb + 1):
                        last = pe.transpose(ps[:, WT_BANKS[qb], at + kb * P:at + (kb + 1) * P],
                                            probs[:, qb % 2, 0, kb * P:(kb + 1) * P], ident[:, :])
                last.then_inc(wt_ps, len(qbs))

            def statistics_of_o(bank, o):
                pe.wait_ge(o_sq, o + 1)
                for tb in range(TB):
                    last = pe.matmul(ps[:, bank, 16 + tb:17 + tb], sqbuf[:, tb * P:(tb + 1) * P],
                                     ones[:, 0:1], start=True, stop=True)
                return last

            def statistics_of_qk(bank, c):
                pe.wait_ge(q_sq, c + 1)
                pe.wait_ge(k_sq, c + 1)
                for j in range(2):
                    for tb in range(TB):
                        last = pe.matmul(ps[:, bank, 4 * tb + 2 * j:4 * tb + 2 * j + 2],
                                         sq_qk[:, j, tb * P:(tb + 1) * P], halves[:, :],
                                         start=True, stop=True)
                return last

            def spread_k(c):
                pe.wait_ge(qk_diag, c + 1)
                for j in range(2):
                    last = pe.matmul(ps[j * HD:(j + 1) * HD, K_SPREAD_BANK, :], ones[:, 0:HD],
                                     sq_qk[:, j, :], start=True, stop=True)
                last.then_inc(qk_spread, 1)

            def spread_o(o):
                pe.wait_ge(o_diag, o + 1)
                pe.matmul(ps[:, O_SPREAD_BANK, :], ones[:, :], obuf[:, :], start=True,
                          stop=True).then_inc(o_spread, 1)

            def pool_product(g):
                pe.wait_ge(wpool_ready, 1)
                pe.wait_ge(pooled_ready, g + 1)
                product(ps[:, POOL_BANK, :], hb(WPOOL, g * P, (g + 1) * P), hb(POOLED), True,
                        True).then_inc(pool_ps, 1)

            def weigh_values(hd):
                pe.wait_ge(wt_ready, 4 * (hd + 1))
                for kb in range(TB):
                    last = product(ps[:, O_BANK, kb * P:T], hb(V0 + kb, hd * P, (hd + 1) * P),
                                   hb(WT0 + kb, kb * P, T), kb == 0, kb == TB - 1)
                last.then_inc(o_ps, 1)

            def even_mixer():
                r0 = start["even"]
                for s in range(RING):
                    pe.wait_ge(lo_done, RING * r0 + s + 1)
                    for j in range(2):
                        k = 2 * s + j
                        pe.wait_ge(gx_ready, NB + k + 1)
                        for tb in range(TB):
                            if k == 0 and V_BANK + tb in RES_BANKS:
                                pe.wait_ge(x_new, 2 * NB + V_BANK + tb - RES_BANKS[1])
                            last = product(ps[:, V_BANK + tb, :], gxb(k, tb * P, (tb + 1) * P),
                                           weight(s, j, T), k == 0, k == NB - 1)
                    last.then_inc(w_used, 1)
                mixer_norm_stats()

                def unit_of(n):
                    return r0 + 1 + n // RING, n % RING

                for c in range(HEADS + 1):
                    p, o = c - 1, c - 2
                    last_stage = c == HEADS
                    if c == 1:
                        pe.wait_ge(u_taken, 1)
                        part_column_block(*unit_of(3), Q_BANK, 0, 3)
                    if p >= 0:
                        pe.wait_ge(k_ready, p + 1)
                        scores(p, 0)
                        if o >= 1:
                            pe.wait_ge(o_scaled, o)
                            pe.wait_ge(pool_ready, o + 1)
                        elif o == 0:
                            pe.wait_ge(pool_ready, 1)
                        scores(p, 1)
                    if not last_stage:
                        if c == 1:
                            part_column_block(*unit_of(3), Q_BANK, 3, NB)
                        else:
                            if c:
                                pe.wait_ge(u_taken, c)
                            column_block(*unit_of(3 * c), Q_BANK)
                    else:
                        pe.wait_ge(u_taken, HEADS)
                        output_split("even_out", 0)
                        pe.wait_ge(y_ready, HEADS - 2)
                        output_part("even_out", 0, EVEN_TILE_BANKS[0], (4, 5, 6, 0, 1))
                    if c == 0:
                        mixer_norm_spread()
                    if p >= 0:
                        if p:
                            pe.wait_ge(wt_ready, 4 * p)
                        transpose_weights(p, 0, 1)
                        scores(p, 2)
                        scores(p, 3)
                    if not last_stage:
                        column_block(*unit_of(3 * c + 1), K_BANK)
                    else:
                        output_split("even_out", 1)
                        output_part("even_out", 1, EVEN_TILE_BANKS[1], (4, 5, 6, 0, 1))
                    if o >= 0:
                        pe.wait_ge(exp_done, 4 * p + 3)
                        stats = statistics_of_o(HEAD_STAT_BANK, o)
                    if last_stage:
                        stats.then_inc(head_stats, 1)
                        output_split("even_out", 2)
                        output_part("even_out", 2, EVEN_TILE_BANKS[2], (4, 5, 6))
                    if p >= 0:
                        if p:
                            pe.wait_ge(o_taken, p)
                        transpose_weights(p, 2)
                        pe.wait_ge(wt_ready, 4 * p + 2)
                        transpose_weights(p, 3)
                    else:
                        pe.wait_ge(v_ready, TB)
                    if c == 0:
                        pe.wait_ge(q_taken, 1)
                        pe.wait_ge(q_sq, 1)
                        part_column_block(*unit_of(2), U_BANK, 0, 2)
                    if not last_stage:
                        statistics_of_qk(HEAD_STAT_BANK, c).then_inc(head_stats, 1)
                        pe.wait_ge(q_taken, c + 1)
                        if c:
                            column_block(*unit_of(3 * c + 2), U_BANK)
                        else:
                            part_column_block(*unit_of(2), U_BANK, 2, NB)
                        spread_k(c)
                    else:
                        output_part("even_out", 2, EVEN_TILE_BANKS[2], (0, 1))
                    if o >= 0:
                        spread_o(o)
                    if p >= 0:
                        pool_product(p)
                        weigh_values(p)
                output_split("even_out", 3)
                pe.wait_ge(head_ms, HEADS + 1)
                output_part("even_out", 3, EVEN_TILE_BANKS[3], (4, 5, 6))
                statistics_of_o(O_STAT_BANK, HEADS - 1).then_inc(head_stats, 1)
                pe.wait_ge(pool_ready, HEADS)
                pe.wait_ge(y_ready, HEADS - 1)
                for m in range(2):
                    output_part("even_out", m, EVEN_TILE_BANKS[m], (7, 2))
                spread_o(HEADS - 1)
                output_part("even_out", 2, EVEN_TILE_BANKS[2], (7, 2))
                output_part("even_out", 3, EVEN_TILE_BANKS[3], (0, 1, 7, 2))
                pe.wait_ge(y_ready, HEADS)
                for m in range(NB):
                    if m >= RING:
                        output_split("even_out", m)
                    output_part("even_out", m, EVEN_TILE_BANKS[m], (3,) if m < RING else (4, 5, 6, 7, 0, 1, 2, 3),
                                end=True)

            def odd_mixer():
                r0 = start["odd"]

                def two_groups(i, first=False):
                    for s in range(2):
                        if not first:
                            pe.wait_ge(group_taken, 2 * i + s - 1)
                        if first and s == 1:
                            pe.wait_ge(norm_ms, 5)
                        for q in range(RING):
                            pe.wait_ge(lo_done, RING * (r0 + 2 * i + s) + q + 1)
                            for j in range(2):
                                k = 2 * q + j
                                if first and s == 0:
                                    pe.wait_ge(gx_ready, 4 * NB + k + 1)
                                for kind in range(3):
                                    last = product(ps[:, GROUP_BANKS[s][kind], :], weight(q, 3 * j + kind), gxb(k),
                                                   k == 0, k == NB - 1)
                            last.then_inc(w_used, 1)
                            if first and s == 0 and q == 1:
                                sum_of_norm(4)

                two_groups(0, True)
                with pe.Fori(1, NB // 2) as i:
                    two_groups(i)
                pe.wait_ge(conv_ready, NB - 1)
                early, every = (4, 5, 6, 0, 1, 2, 3), (4, 5, 6, 7, 0, 1, 2, 3)
                for m in range(2):
                    pe.wait_ge(x_new, 5 * NB + m - 1)
                    output_split("odd_out", m)
                    output_part("odd_out", m, RES_BANKS[m], early)
                pe.wait_ge(conv_ready, NB)
                for m in range(NB):
                    if m >= 2:
                        pe.wait_ge(x_new, 5 * NB + m - 1)
                        output_split("odd_out", m)
                    output_part("odd_out", m, RES_BANKS[m % 2], (7,) if m < 2 else every, end=True)

            pe.wait_ge(consts, 9)
            pe.wait_ge(first_gains_in, 16)
            pe.transpose(ps[:, SPREAD_BANK, 0:NB], rows[0:NB, :], ident[0:NB, 0:NB]).then_inc(cols_ps, 1)
            transpose_x(0)
            ffn(0)
            even_mixer()
            ffn(1)
            ffn(2)
            odd_mixer()
            ffn(3)

        @block.scalar
        def _(act):
            def round_unit(rnd, slot, blocks=NB, first=False, phase=None):
                act.wait_ge(raw_in[slot], loaded(rnd, phase))
                if not first:
                    act.wait_ge(w_used, units_used(rnd - 1, slot))
                act.activation(whi[:, slot, 0:blocks * P], raw[:, slot, 0:blocks * P],
                               ACT.Copy).then_inc(hi_done, 1)

            def residual(phase, m, into=sqbuf, added=None):
                g = NB * phase + m
                act.wait_ge(cols_ready, 2)
                act.wait_ge(x_new, g + 1)
                act.activation(gx[:, m, 0, :], x[:, m, :], ACT.Copy,
                               scale=cols[:, bass.ds(g, 1)]).then_inc(xhi_done, 1)
                act.wait_ge(cols_ready, 2)
                act.wait_ge(sq_added, g if added is None else added)
                act.activation(into[:, :], x[:, m, :], ACT.Square).then_inc(sq_done, 1)

            def root(ms_ready, count, a, b, done):
                act.wait_ge(ms_ready, count)
                act.activation(sd[:, :, a:b], ms[:, :, a:b], ACT.Sqrt).then_inc(done, 1)

            def round_acc(r):
                act.wait_ge(sq_added, NB * (r + 1))
                act.activation(h[:, 0, 0, :], acc[:, :], ACT.Copy).then_inc(acc_hi, 1)

            def norm_roots(r):
                act.wait_ge(norm_ms, r + 1)
                act.activation(obuf[:, :], sqbuf[:, :], ACT.Sqrt).then_inc(norm_root, 1)

            def ffn(f):
                phase = FFNS[f][4]
                r0 = start[f"ffn{f}"]
                r1 = r0 + FT // 2

                def activate(t):
                    act.wait_ge(gate_scaled, FT * f + t + 1)
                    act.activation(gbuf[:, PAD:], gbuf[:, PAD:], ACT.Silu).then_inc(silu_done, 1)
                    act.wait_ge(cols_ready, 1)
                    act.wait_ge(h_new, FT * f + t + 1)
                    act.activation(h[:, t, 0, :], ubuf[:, :], ACT.Copy).then_inc(hhi_done, 1)

                name = f"ffn{f}"

                def two_tiles(i, first=False, at_norm=False):
                    if not first:
                        round_unit(r0 + i, 2, phase=name)
                        round_unit(r0 + i, 3, phase=name)
                    if at_norm:
                        norm_roots(phase - 1)
                        round_unit(r0 + i + 1, 0, phase=name)
                        activate(2 * i)
                    else:
                        activate(2 * i)
                        round_unit(r0 + i + 1, 0, phase=name)
                    round_unit(r0 + i + 1, 1, phase=name)
                    activate(2 * i + 1)

                round_acc(phase - 1)
                two_tiles(0, first=f == 0, at_norm=True)
                with act.Fori(1, FT // 2 - 1) as i:
                    two_tiles(i)
                round_unit(r1 - 1, 2, phase=name)
                round_unit(r1 - 1, 3, phase=name)
                activate(FT - 2)
                for s in range(RING):
                    round_unit(r1, s, DOWN_UNITS[s], phase=name)
                activate(FT - 1)
                if f == 0:
                    act.wait_ge(lam_sum_ready, 1)
                    act.activation(lam_exp[:, :], lam_sum[:, :], ACT.Exp).then_inc(lam_exp_ready, 1)

                def next_tile(m):
                    for s in range(RING):
                        round_unit(r1 + m + 1, s, DOWN_UNITS[s], phase=name)

                if f < 3:
                    with act.Fori(0, NB - 1) as m:
                        next_tile(m)
                        residual(phase, m)
                else:
                    next_tile(0)
                    for s in range(2):
                        next_tile(s + 1)
                        store_result(s, s, first=True)
                    with act.Fori(1, NB // 2 - 1) as i:
                        for s in range(2):
                            next_tile(2 * i + s + 1)
                            store_result(2 * i + s, s)
                    store_result(NB - 2, 0)
                    store_result(NB - 1, 1)
                if f < 3:
                    blocks = 6 if f == 2 else NB
                    after = "odd" if f == 2 else None
                    round_unit(r1 + NB, 0, blocks, phase=after)
                    round_unit(r1 + NB, 1, blocks, phase=after)
                    residual(phase, NB - 1)

            def out_projection(name, phase, ahead):
                for m in range(NB):
                    if m + ahead < NB + 2:
                        round_unit(start[name] + (m + ahead) // RING, (m + ahead) % RING, phase=name)
                    residual(phase, m, squares(m), NB * phase + max(m - 1, 0))

            def store_result(m, s, first=False):
                act.wait_ge(outT_ps, m + 1)
                if not first:
                    act.wait_ge(stored[s], 8 * m - 8 * s)
                act.activation(probs[:, s, 0, :], ps[:, OUT_BANKS[s], :], ACT.Copy).then_inc(outT_copied, 1)
                act.wait_ge(outT_copied, m + 1)
                act.dma_start(out[0].rearrange("(b p) d -> p b d", p=P)[:, :, bass.ds(m * P, P)],
                              probs[:, s, 0, :].rearrange("p (b n) -> p b n", b=TB)).then_inc(stored[s], 16)

            def exps(hd, qb):
                act.wait_ge(bias_ready, 4 * hd + qb + 1)
                if 4 * hd + qb >= 2:
                    act.wait_ge(wt_ps, 4 * hd + qb - 1)
                for c in range(2):
                    last = act.activation(probs[:, qb % 2, c, 0:(qb + 1) * P],
                                          ps[:, SCORE_BANKS[qb % 2] + c, 0:(qb + 1) * P], ACT.Exp,
                                          scale=qscale[:, qb, c:c + 1], bias=nbias[:, qb % 2, c:c + 1],
                                          accum_out=sums[:, qb % 2, c:c + 1])
                last.then_inc(exp_done, 1)

            def round_weights(hd, *qbs):
                act.wait_ge(wt_ps, 4 * hd + qbs[-1] + 1)
                if qbs[0] == 0 and hd:
                    act.wait_ge(o_ps, hd)
                for qb in qbs:
                    at = P if qb == 1 else 0
                    last = act.activation(h[:, WT0:WT0 + qb + 1, 0, qb * P:(qb + 1) * P],
                                          ps[:, WT_BANKS[qb], at:at + (qb + 1) * P].rearrange(
                                              "p (k n) -> p k n", n=P), ACT.Copy)
                last.then_inc(wt_hi, len(qbs))

            def even_mixer():
                r0 = start["even"]

                def round_unit_of(n):
                    round_unit(r0 + 1 + n // RING, n % RING)

                round_unit(r0, 2)
                round_unit(r0, 3)
                round_unit_of(0)
                round_unit_of(1)
                root(norm_ms, 2, 0, 1, norm_root)
                act.wait_ge(norm_diag, 1)
                for tb in range(TB):
                    act.activation(h[:, V0 + tb, 0, :], ps[:, V_BANK + tb, :], ACT.Copy,
                                   scale=Rc[:, tb:tb + 1]).then_inc(v_hi, 1)
                for c in range(HEADS + 1):
                    p, o = c - 1, c - 2
                    if p >= 0:
                        exps(p, 0)
                        exps(p, 1)
                    if c < HEADS:
                        round_unit_of(3 * c + 2)
                        act.wait_ge(w_used, units_used(r0 + 1, 3 * c))
                        act.activation(h[:, Q0 + c % 2, 0, :], ps[:, Q_BANK, :], ACT.Copy,
                                       scale=cols[:, COL_QGAIN:COL_QGAIN + 1]).then_inc(q_hi, 1)
                    else:
                        round_unit_of(3 * c + 2)
                        round_unit_of(3 * c + 3)
                    if c == 0:
                        act.wait_ge(wpool_in, 16)
                        act.activation(h[:, WPOOL, 0, :], acc[:, :], ACT.Copy).then_inc(wpool_hi, 1)
                    if p >= 0:
                        round_weights(p, 0, 1)
                    if c < HEADS:
                        if c:
                            act.wait_ge(qk_spread, c)
                        act.wait_ge(q_taken, c + 1)
                        act.activation(sq_qk[:, 0, :], ps[:, Q_BANK, :], ACT.Square).then_inc(q_sq, 1)
                        round_unit_of(3 * c + 3)
                    if p >= 0:
                        exps(p, 2)
                        if c < HEADS:
                            round_pooled(p)
                        exps(p, 3)
                    if c < HEADS:
                        round_unit_of(3 * c + 4)
                        act.wait_ge(w_used, units_used(r0 + 1, 3 * c + 1))
                        if c:
                            act.wait_ge(k_ready, c)
                        act.activation(ubuf[:, :], ps[:, K_BANK, :], ACT.Copy,
                                       scale=cols[:, COL_KGAIN:COL_KGAIN + 1]).then_inc(k_taken, 1)
                        act.activation(sq_qk[:, 1, :], ps[:, K_BANK, :], ACT.Square).then_inc(k_sq, 1)
                    if c == HEADS:
                        root(head_ms, c + 1, 4, 5, head_root)
                    if p >= 0:
                        round_weights(p, 2)
                        round_weights(p, 3)
                    if c < HEADS:
                        root(head_ms, c + 1, 0, 5 if o >= 0 else 4, head_root)
                    else:
                        round_pooled(p)
                    if c < HEADS:
                        act.wait_ge(k_scaled, c + 1)
                        act.activation(h[:, K0, 0, :], ubuf[:, :], ACT.Copy).then_inc(k_hi, 1)
                    if o >= 0:
                        round_y(o)
                    if p >= 0:
                        act.wait_ge(pool_ps, p + 1)
                        act.activation(h[:, Y0 + HEADS + p, 0, :], ps[:, POOL_BANK, :], ACT.Copy,
                                       scale=cols[:, COL_PSCALE + p:COL_PSCALE + p + 1]).then_inc(pool_hi, 1)
                        act.wait_ge(o_ps, p + 1)
                        act.activation(sqbuf[:, :], ps[:, O_BANK, :], ACT.Square).then_inc(o_sq, 1)
                        if o >= 0:
                            act.wait_ge(y_ready, o + 1)
                        act.activation(acc[:, :], ps[:, O_BANK, :], ACT.Copy,
                                       scale=sub_gain[:, 0:1]).then_inc(o_taken, 1)
                root(head_ms, HEADS + 2, 4, 5, head_root)
                round_y(HEADS - 1)
                out_projection("even_out", 2, ahead=4)

            def round_pooled(g):
                act.wait_ge(pooled_new, g + 1)
                act.activation(h[:, POOLED, 0, :], pooled(g), ACT.Copy).then_inc(pooled_hi, 1)

            def round_y(o):
                act.wait_ge(o_scaled, o + 1)
                act.activation(h[:, Y0 + o, 0, :], acc[:, :], ACT.Copy).then_inc(y_hi, 1)

            def odd_mixer():
                r0 = start["odd"]

                def group(g, next_blocks=6, stats=False, following="odd"):
                    if stats:
                        round_acc(4)
                        round_unit(r0, 2, 6, phase="odd")
                        round_unit(r0, 3, 6, phase="odd")
                        norm_roots(4)
                    for slot in range(RING if following == "odd" else 2):
                        round_unit(r0 + g + 1, slot, next_blocks, phase=following)
                    act.wait_ge(cols_ready, 1)
                    act.wait_ge(conv_new, g + 1)
                    act.activation(h[:, Y0 + g, 0, :], obuf[:, :], ACT.Copy).then_inc(conv_hi, 1)

                group(0, stats=True)
                with act.Fori(1, NB - 1) as g:
                    group(g)
                group(NB - 1, next_blocks=NB, following="odd_out")
                out_projection("odd_out", 5, ahead=2)

            act.wait_ge(cols_ps, 1)
            act.activation(cols[:, 0:NB], ps[:, SPREAD_BANK, 0:NB], ACT.Copy).then_inc(cols_ready, 1)
            act.wait_ge(cols_ready, 1)
            for kind, m in FIRST_STEPS:
                if kind == "unit":
                    round_unit(0, m, first=True)
                elif kind == "x":
                    act.wait_ge(x_new, m + 1)
                    act.activation(gx[:, m, 0, :], x[:, m, :], ACT.Copy,
                                   scale=cols[:, m:m + 1]).then_inc(xhi_done, 1)
                else:
                    if m >= 2:
                        act.wait_ge(sq_added, m - 1)
                    act.activation(squares(m)[:, :], x[:, m, :], ACT.Square).then_inc(sq_done, 1)
            ffn(0)
            even_mixer()
            ffn(1)
            ffn(2)
            odd_mixer()
            ffn(3)

        @block.vector
        def _(dve):
            steps = [0]

            def then(instruction):
                steps[0] += 1
                instruction.then_inc(step, 1)
                dve.wait_ge(step, steps[0])

            def split_unit(rnd, slot, blocks=NB):
                dve.wait_ge(hi_done, RING * rnd + slot + 1)
                dve.tensor_tensor(wlo[:, slot, 0:blocks * P], raw[:, slot, 0:blocks * P],
                                  whi[:, slot, 0:blocks * P], ALU.subtract).then_inc(lo_done, 1)

            def rest_of_gx(phase, m):
                g = NB * phase + m
                dve.wait_ge(xhi_done, g + 1)
                dve.wait_ge(x_new, g + 1)
                dve.scalar_tensor_tensor(gx[:, m, 1, :], x[:, m, :], cols[:, bass.ds(g, 1)],
                                         gx[:, m, 0, :], ALU.mult, ALU.subtract).then_inc(gx_ready, 1)

            def add_tile(phase, m, bank, coefficient, ready, count):
                dve.wait_ge(ready, count)
                dve.scalar_tensor_tensor(x[:, m, :], ps[:, bank, :], coefficient, x[:, m, :],
                                         ALU.mult, ALU.add).then_inc(x_new, 1)

            def split_block(phase, m, squared=sqbuf):
                g = NB * phase + m
                rest_of_gx(phase, m)
                dve.wait_ge(sq_done, g + 1)
                dve.wait_ge(sq_added, g)
                dve.tensor_tensor(acc[:, :], acc[:, :], squared[:, :], ALU.add).then_inc(sq_added, 1)

            def clear_acc():
                then(dve.memset(acc[:, :], 0.0))

            def newton(a, b, c, d, ms_done, root_done, count):
                dve.wait_ge(ms_done, count)
                dve.wait_ge(root_done, count)
                then(dve.reciprocal(a, d))
                then(dve.tensor_tensor(b, a, a, ALU.mult))
                then(dve.tensor_tensor(b, b, c, ALU.mult))
                then(dve.tensor_scalar(b, b, -0.5, 1.5, ALU.mult, ALU.add))
                return dve.tensor_tensor(a, a, b, ALU.mult)

            def inverse_root(first, end, ms_done, root_done, count):
                then(newton(*(buf[:, :, first:end] for buf in (rs, nt, ms, sd)), ms_done, root_done, count))

            def diagonal(dst, factors):
                return dve.tensor_tensor(dst.rearrange("p (b n) -> p b n", b=TB),
                                         ident[:, :].unsqueeze(1).to_broadcast([P, TB, P]),
                                         factors.to_broadcast([P, TB, P]), ALU.mult)

            def split_acc(r):
                dve.wait_ge(acc_hi, wide_norms(r))
                dve.tensor_tensor(h[:, 0, 1, :], acc[:, :], h[:, 0, 0, :], ALU.subtract).then_inc(acc_lo, 1)

            def norm_squares(r):
                dve.wait_ge(norm_spread, r + 1)
                dve.tensor_scalar(sqbuf[:, :], ps[:, SPREAD_BANK, :], 1.0 / D, EPS, ALU.mult,
                                  ALU.add).then_inc(norm_ms, 1)

            def norm_factors(r):
                newton(R[:, :], ubuf[:, :], sqbuf[:, :], obuf[:, :], norm_ms, norm_root,
                       r + 1).then_inc(norm_ready, 1)
                dve.wait_ge(norm_ready, r + 1)

            def mixer_norm_factors():
                dve.wait_ge(norm_stats, 1)
                dve.tensor_scalar(ms[:, :, 0:1], ps[:, STAT_BANK, 0:TB].unsqueeze(2), 1.0 / D, EPS,
                                  ALU.mult, ALU.add).then_inc(norm_ms, 1)
                inverse_root(0, 1, norm_ms, norm_root, 2)
                then(dve.tensor_copy(Rc[:, :].unsqueeze(2), rs[:, :, 0:1]))
                diagonal(obuf[:, :], Rc[:, :].unsqueeze(2)).then_inc(norm_diag, 1)

            def mixer_norm_rows():
                dve.wait_ge(norm_spread, 2)
                dve.tensor_copy(R[:, :], ps[:, SPREAD_BANK, :]).then_inc(norm_ready, 1)
                dve.wait_ge(norm_ready, 2)

            def ffn(f):
                phase = FFNS[f][4]
                r0 = start[f"ffn{f}"]
                r1 = r0 + FT // 2

                def hidden(t, s):
                    dve.wait_ge(w_used, RING * r0 + 2 * t + 2)
                    dve.tensor_tensor(gbuf[:, PAD:], ps[:, GATE_BANKS[s], :], R[:, :],
                                      ALU.mult).then_inc(gate_scaled, 1)
                    dve.wait_ge(h_ready, FT * f + t)
                    dve.tensor_tensor(ubuf[:, :], ps[:, GATE_BANKS[s] + 1, :], R[:, :],
                                      ALU.mult).then_inc(up_scaled, 1)
                    dve.wait_ge(silu_done, FT * f + t + 1)
                    dve.wait_ge(up_scaled, FT * f + t + 1)
                    dve.tensor_tensor(ubuf[:, :], gbuf[:, PAD:], ubuf[:, :], ALU.mult).then_inc(h_new, 1)
                    dve.wait_ge(hhi_done, FT * f + t + 1)
                    dve.tensor_tensor(h[:, t, 1, :], ubuf[:, :], h[:, t, 0, :],
                                      ALU.subtract).then_inc(h_ready, 1)

                def two_tiles(i):
                    split_unit(r0 + i, 2)
                    split_unit(r0 + i, 3)
                    hidden(2 * i, 0)
                    split_unit(r0 + i + 1, 0)
                    split_unit(r0 + i + 1, 1)
                    hidden(2 * i + 1, 1)

                split_acc(phase - 1)
                norm_squares(phase - 1)
                if f:
                    split_unit(r0, 2)
                    split_unit(r0, 3)
                norm_factors(phase - 1)
                split_unit(r0 + 1, 0)
                hidden(0, 0)
                split_unit(r0 + 1, 1)
                hidden(1, 1)
                with dve.Fori(1, FT // 2 - 1) as i:
                    two_tiles(i)
                split_unit(r1 - 1, 2)
                split_unit(r1 - 1, 3)
                hidden(FT - 2, 0)
                for s in range(RING):
                    split_unit(r1, s, DOWN_UNITS[s])
                hidden(FT - 1, 1)
                clear_acc()
                if f == 0:
                    dve.wait_ge(lam_in, 4 * 16)
                    then(dve.tensor_tensor(lam_prod[:, :, :], lam_rows[:, 0:2, :], lam_rows[:, 2:4, :],
                                           ALU.mult))
                    dve.reduce_sum(lam_sum[:, :], lam_prod[:, :, :], AX_X).then_inc(lam_sum_ready, 1)
                    dve.memset(lam_pair[:, 0:1], 1.0)
                    dve.wait_ge(lam_exp_ready, 1)
                    then(dve.tensor_tensor(lam_pair[:, 1:2], lam_exp[:, 1:2], lam_exp[:, 0:1], ALU.subtract))
                    then(dve.tensor_scalar(lam_pair[:, 1:2], lam_pair[:, 1:2], -LAM_INIT, None, ALU.add))

                def next_tile(m):
                    for s in range(RING):
                        split_unit(r1 + m + 1, s, DOWN_UNITS[s])

                def down_result(m, s, first=False):
                    dve.wait_ge(w_used, units_used(r1 + m, RING - 1))
                    if not first:
                        dve.wait_ge(outT_ps, m - 1)
                    dve.scalar_tensor_tensor(fin(s)[:, :], ps[:, RES_BANKS[s], :], 0.5, x[:, m, :],
                                             ALU.mult, ALU.add).then_inc(fin_ready, 1)

                def down_residual(m, s):
                    add_tile(phase, m, RES_BANKS[s], 0.5, w_used, units_used(r1 + m, RING - 1))
                    split_block(phase, m)

                if f < 3:
                    with dve.Fori(0, NB // 2 - 1) as i:
                        for s in range(2):
                            next_tile(2 * i + s)
                            down_residual(2 * i + s, s)
                    next_tile(NB - 2)
                    down_residual(NB - 2, 0)
                    blocks = 6 if f == 2 else NB
                    split_unit(r1 + NB, 0, blocks)
                    split_unit(r1 + NB, 1, blocks)
                    down_residual(NB - 1, 1)
                else:
                    for m in range(2):
                        next_tile(m)
                        down_result(m, m, first=True)
                    with dve.Fori(1, NB // 2 - 1) as i:
                        for s in range(2):
                            next_tile(2 * i + s)
                            down_result(2 * i + s, s)
                    next_tile(NB - 2)
                    down_result(NB - 2, 0)
                    down_result(NB - 1, 1)

            def out_projection(name, phase, banks, ahead):
                def split_ahead(m):
                    if m + ahead < NB + 2:
                        split_unit(start[name] + (m + ahead) // RING, (m + ahead) % RING)

                for m in range(NB):
                    if ahead < RING:
                        split_ahead(m)
                    add_tile(phase, m, banks[m], 1.0, w_used, units_used(start[name], m))
                    if ahead == RING:
                        split_ahead(m)
                    if m:
                        split_block(phase, m - 1, squares(m - 1))
                split_block(phase, NB - 1, squares(NB - 1))

            def row_maxima(hd, qb):
                n = (qb + 1) * P
                pair = ps[:, SCORE_BANKS[qb % 2]:SCORE_BANKS[qb % 2] + 2, :]
                dve.wait_ge(scores_ready, 4 * hd + qb + 1)
                then(dve.tensor_tensor(pair[:, :, n - P:n], pair[:, :, n - P:n],
                                       mask[:, :].unsqueeze(1).to_broadcast([P, 2, P]), ALU.add))
                then(dve.reduce_max(mx[:, qb % 2, :], pair[:, :, 0:n], AX_X))
                dve.tensor_tensor(nbias[:, qb % 2, :], mx[:, qb % 2, :], nqscale[:, qb, :],
                                  ALU.mult).then_inc(bias_ready, 1)

            def combine(hd, qb):
                n = (qb + 1) * P
                dve.wait_ge(exp_done, 4 * hd + qb + 1)
                then(dve.reciprocal(rec[:, qb % 2, :], sums[:, qb % 2, :]))
                then(dve.tensor_tensor(rec[:, qb % 2, :], rec[:, qb % 2, :], lam_pair[:, :], ALU.mult))
                then(dve.tensor_scalar(probs[:, qb % 2, 1, 0:n], probs[:, qb % 2, 1, 0:n],
                                       rec[:, qb % 2, 1:2], None, ALU.mult))
                dve.scalar_tensor_tensor(probs[:, qb % 2, 0, 0:n], probs[:, qb % 2, 0, 0:n],
                                         rec[:, qb % 2, 0:1], probs[:, qb % 2, 1, 0:n],
                                         ALU.mult, ALU.add).then_inc(w_ready, 1)

            def split_weights(hd, *qbs):
                dve.wait_ge(wt_hi, 4 * hd + qbs[-1] + 1)
                for qb in qbs:
                    at = P if qb == 1 else 0
                    last = dve.tensor_tensor(h[:, WT0:WT0 + qb + 1, 1, qb * P:(qb + 1) * P],
                                             ps[:, WT_BANKS[qb], at:at + (qb + 1) * P].rearrange(
                                                 "p (k n) -> p k n", n=P),
                                             h[:, WT0:WT0 + qb + 1, 0, qb * P:(qb + 1) * P], ALU.subtract)
                last.then_inc(wt_ready, len(qbs))

            def head_factors(stage, bank, c=None, o=None):
                dve.wait_ge(head_stats, stage + 1)
                if o is not None:
                    last = dve.tensor_scalar(ms[:, :, 4:5], ps[:, bank, 16:16 + TB].unsqueeze(2), 1.0 / P, EPS,
                                             ALU.mult, ALU.add)
                if c is not None:
                    then(dve.tensor_tensor(ms[:, :, 0:4], ps[:, bank, 0:16].rearrange("p (b c) -> p b c", b=TB),
                                           Rc2[:, :].unsqueeze(2).to_broadcast([P, TB, 4]), ALU.mult))
                    last = dve.tensor_scalar(ms[:, :, 0:4], ms[:, :, 0:4], 1.0 / HD, EPS, ALU.mult, ALU.add)
                last.then_inc(head_ms, 1)
                inverse_root(0 if c is not None else 4, 5 if o is not None else 4, head_ms, head_root, stage + 1)
                if c is not None:
                    then(dve.tensor_tensor(rs[:, :, 0:4], rs[:, :, 0:4],
                                           Rc[:, :].unsqueeze(2).to_broadcast([P, TB, 4]), ALU.mult))
                    for j in range(2):
                        last = diagonal(sq_qk[:, j, :], rs[:, :, 2 + j:3 + j])
                    last.then_inc(qk_diag, 1)
                if o is not None:
                    diagonal(obuf[:, :], rs[:, :, 4:5]).then_inc(o_diag, 1)
                if c is not None:
                    dve.tensor_scalar(qscale[:, :, :], rs[:, :, 0:2], HD ** -0.5, None, ALU.mult)
                    then(dve.tensor_scalar(nqscale[:, :, :], rs[:, :, 0:2], -HD ** -0.5, None, ALU.mult))

            def scale_o(o):
                dve.wait_ge(o_taken, o + 1)
                dve.wait_ge(o_spread, o + 1)
                dve.tensor_tensor(acc[:, :], acc[:, :], ps[:, O_SPREAD_BANK, :], ALU.mult).then_inc(o_scaled, 1)

            def rest_of_y(o):
                dve.wait_ge(y_hi, o + 1)
                dve.wait_ge(o_scaled, o + 1)
                dve.tensor_tensor(h[:, Y0 + o, 1, :], acc[:, :], h[:, Y0 + o, 0, :],
                                  ALU.subtract).then_inc(y_ready, 1)

            def even_mixer():
                r0 = start["even"]
                split_unit(r0, 2)
                split_unit(r0, 3)
                split_unit(r0 + 1, 0)
                split_unit(r0 + 1, 1)
                mixer_norm_factors()
                then(dve.tensor_tensor(Rc2[:, :], Rc[:, :], Rc[:, :], ALU.mult))
                for tb in range(TB):
                    dve.wait_ge(v_hi, tb + 1)
                    dve.scalar_tensor_tensor(h[:, V0 + tb, 1, :], ps[:, V_BANK + tb, :], Rc[:, tb:tb + 1],
                                             h[:, V0 + tb, 0, :], ALU.mult, ALU.subtract).then_inc(v_ready, 1)
                for c in range(HEADS + 1):
                    p, o = c - 1, c - 2
                    if p >= 0:
                        row_maxima(p, 0)
                        row_maxima(p, 1)
                        combine(p, 0)
                        combine(p, 1)
                    if c == HEADS:
                        dve.wait_ge(lo_done, RING * start["even_out"] + 2)
                        split_unit(start["even_out"], 2)
                        split_unit(start["even_out"], 3)
                    if c < HEADS:
                        dve.wait_ge(q_hi, c + 1)
                        dve.scalar_tensor_tensor(h[:, Q0 + c % 2, 1, :], ps[:, Q_BANK, :],
                                                 cols[:, COL_QGAIN:COL_QGAIN + 1], h[:, Q0 + c % 2, 0, :],
                                                 ALU.mult, ALU.subtract).then_inc(q_taken, 1)
                    if c == 0:
                        mixer_norm_rows()
                        dve.wait_ge(wpool_hi, 1)
                        dve.tensor_tensor(h[:, WPOOL, 1, :], acc[:, :], h[:, WPOOL, 0, :],
                                          ALU.subtract).then_inc(wpool_ready, 1)
                    if p >= 0:
                        split_weights(p, 0, 1)
                        row_maxima(p, 2)
                        row_maxima(p, 3)
                        combine(p, 2)
                        combine(p, 3)
                    if c == HEADS:
                        head_factors(c, HEAD_STAT_BANK, o=o)
                    if p >= 0:
                        split_weights(p, 2)
                        split_weights(p, 3)
                    if c < HEADS:
                        head_factors(c, HEAD_STAT_BANK, c=c, o=o if o >= 0 else None)
                    if c < HEADS:
                        dve.wait_ge(w_used, units_used(r0 + 1, 3 * c + 2))
                        if c:
                            dve.wait_ge(pooled_new, c)
                        dve.tensor_tensor(tbuf[:, PAD:], ps[:, U_BANK, :], R[:, :], ALU.mult).then_inc(u_taken, 1)
                        dve.wait_ge(k_taken, c + 1)
                        dve.wait_ge(qk_spread, c + 1)
                        dve.tensor_tensor(ubuf[:, :], ubuf[:, :], ps[:, K_SPREAD_BANK, :],
                                          ALU.mult).then_inc(k_scaled, 1)
                    if o >= 0:
                        scale_o(o)
                    if c < HEADS:
                        dve.wait_ge(k_hi, c + 1)
                        dve.tensor_tensor(h[:, K0, 1, :], ubuf[:, :], h[:, K0, 0, :],
                                          ALU.subtract).then_inc(k_ready, 1)
                    if o >= 0:
                        rest_of_y(o)
                    if p >= 0:
                        dve.wait_ge(pool_hi, p + 1)
                        dve.scalar_tensor_tensor(h[:, Y0 + HEADS + p, 1, :], ps[:, POOL_BANK, :],
                                                 cols[:, COL_PSCALE + p:COL_PSCALE + p + 1],
                                                 h[:, Y0 + HEADS + p, 0, :],
                                                 ALU.mult, ALU.subtract).then_inc(pool_ready, 1)
                head_factors(HEADS + 1, O_STAT_BANK, o=HEADS - 1)
                scale_o(HEADS - 1)
                rest_of_y(HEADS - 1)
                dve.wait_ge(y_ready, HEADS)
                clear_acc()
                out_projection("even_out", 2, EVEN_TILE_BANKS, ahead=RING)

            def odd_mixer():
                r0 = start["odd"]

                def group(g, s, next_blocks=6, stats=False, more=True):
                    banks = GROUP_BANKS[s]
                    if stats:
                        split_acc(4)
                        split_unit(r0, 2, 6)
                        split_unit(r0, 3, 6)
                        norm_squares(4)
                    split_unit(r0 + g + 1, 0, next_blocks)
                    split_unit(r0 + g + 1, 1, next_blocks)
                    if stats:
                        norm_factors(4)
                    dve.wait_ge(w_used, units_used(r0 + g, RING - 1))
                    dve.tensor_tensor(gbuf[:, PAD:], ps[:, banks[1], :], R[:, :], ALU.mult)
                    dve.tensor_tensor(ubuf[:, :], ps[:, banks[2], :], R[:, :], ALU.mult).then_inc(conv_step, 1)
                    dve.tensor_tensor(obuf[:, :], ps[:, banks[0], :], R[:, :], ALU.mult).then_inc(group_taken, 1)
                    dve.wait_ge(conv_step, 5 * g + 1)
                    dve.tensor_tensor(zbuf[:, PAD:], gbuf[:, PAD:], ubuf[:, :], ALU.mult).then_inc(conv_step, 1)
                    dve.wait_ge(conv_step, 5 * g + 2)
                    if more:
                        split_unit(r0 + g + 1, 2, 6)
                    for j in range(CONV):
                        shifted = zbuf[:, PAD - (CONV - 1 - j):PAD - (CONV - 1 - j) + T]
                        tap = cols[:, bass.ds(g + (COL_CONV + NB * j), 1)]
                        if j == 0:
                            dve.tensor_scalar(sqbuf[:, :], shifted, tap, None, ALU.mult).then_inc(conv_step, 1)
                        else:
                            dve.scalar_tensor_tensor(sqbuf[:, :], shifted, tap, sqbuf[:, :], ALU.mult,
                                                     ALU.add).then_inc(conv_step, 1)
                        dve.wait_ge(conv_step, 5 * g + 3 + j)
                    dve.tensor_tensor(obuf[:, :], obuf[:, :], sqbuf[:, :], ALU.mult).then_inc(conv_new, 1)
                    dve.wait_ge(conv_hi, g + 1)
                    dve.tensor_tensor(h[:, Y0 + g, 1, :], obuf[:, :], h[:, Y0 + g, 0, :],
                                      ALU.subtract).then_inc(conv_ready, 1)
                    if more:
                        split_unit(r0 + g + 1, 3, 6)

                group(0, 0, stats=True)
                group(1, 1)
                with dve.Fori(1, NB // 2 - 1) as i:
                    group(2 * i, 0)
                    group(2 * i + 1, 1)
                group(NB - 2, 0)
                group(NB - 1, 1, next_blocks=NB, more=False)
                clear_acc()
                out_projection("odd_out", 5, RES_BANKS * (NB // 2), ahead=2)

            def copy_block(m):
                dve.wait_ge(xT_ps, m + 1)
                dve.tensor_copy(x[:, m, :], ps[:, m, :]).then_inc(x_new, 1)

            for kind, m in FIRST_STEPS:
                if kind == "unit":
                    split_unit(0, m)
                elif kind == "x":
                    if m % (NB // 2) == 0:
                        copy_block(m)
                        copy_block(m + 1)
                    if m % (NB // 2) < NB // 2 - 2:
                        copy_block(m + 2)
                    rest_of_gx(0, m)
            dve.wait_ge(cols_ps, 2)
            dve.tensor_copy(cols[:, NB:N_COLS], ps[:, SPREAD_BANK, NB:N_COLS]).then_inc(cols_ready, 1)
            dve.tensor_copy(ones_r[:, :], ones[:, :])
            dve.wait_ge(cols_ready, 2)
            dve.tensor_scalar(sub_gain[:, :], cols[:, COL_SUB:COL_SUB + 1], 1.0 - LAM_INIT, None, ALU.mult)
            ffn(0)
            even_mixer()
            ffn(1)
            ffn(2)
            odd_mixer()
            ffn(3)


_INS = ["x", "ffn1_norm", "ffn1_w_gate", "ffn1_w_up", "ffn1_w_down", "ffn2_norm", "ffn2_w_gate", "ffn2_w_up",
        "ffn2_w_down", "mix_norm", "even_w_in", "even_w_out", "q_gain", "k_gain", "subln_gain", "lambda_q1",
        "lambda_k1", "lambda_q2", "lambda_k2", "w_pool", "pool_scale", "odd_w_in", "conv_w", "odd_w_out"]
_OUT = ((1, T, D), "float32")


def kernel(**inputs):
    import numpy as _np
    import concourse.bacc as _bacc
    from concourse import mybir as _mybir
    from concourse.bass_utils import run_bass_kernel_spmd as _run

    nc = _bacc.Bacc("TRN2", target_bir_lowering=False, num_devices=1,
                    dynamic_dma_scratch_size=2048)
    arrays, args = {}, []
    for name in _INS:
        a = _np.ascontiguousarray(inputs[name])
        arrays[f"in_{name}"] = a
        args.append(nc.dram_tensor(f"in_{name}", a.shape, _mybir.dt.from_np(a.dtype), kind="ExternalInput").ap())
    shape, dtype = _OUT
    out = nc.dram_tensor("out", shape, _mybir.dt.from_np(_np.dtype(dtype)), kind="ExternalOutput").ap()
    build(nc, *args, out)
    r = _run(nc, [arrays], core_ids=[0])
    return r.results[0]["out"]
```
